# Optimizing a Trainium2 kernel written in Bass

```python
import jax, jax.numpy as jnp
from jax import lax
import numpy as np

D_MODEL = 1024
BATCH = 1
SEQ = 256
DEPTH = 2

N_A_LAYERS = DEPTH // 2
N_B_LAYERS = DEPTH - N_A_LAYERS

POOL_WINDOWS = (2, 4, 8, 16)
N_POOL_GROUPS = len(POOL_WINDOWS)
POOL_GROUP = D_MODEL // N_POOL_GROUPS

N_HEADS = 16
QK_NOPE_DIM = 128
QK_ROPE_DIM = 64
QK_DIM = QK_NOPE_DIM + QK_ROPE_DIM
V_DIM = 128
Q_LORA_RANK = 256
KV_LORA_RANK = 128
ROPE_THETA = 10000.0
Q_BLOCK = 128

D_FF = 2816
RMS_EPS = 1e-6


def rmsnorm(x, g):
    xf = x.astype(jnp.float32)
    y = xf * lax.rsqrt(jnp.mean(xf * xf, axis=-1, keepdims=True) + RMS_EPS)
    return (y * g.astype(jnp.float32)).astype(x.dtype)

def swiglu(u, wg, wu, wd):
    return (jax.nn.silu(u @ wg) * (u @ wu)) @ wd

def rope_tables(seq):
    pos = jnp.arange(seq, dtype=jnp.float32)
    inv_freq = ROPE_THETA ** (-jnp.arange(0, QK_ROPE_DIM, 2, dtype=jnp.float32) / QK_ROPE_DIM)
    ang = pos[:, None] * inv_freq[None, :]
    return jnp.cos(ang), jnp.sin(ang)

def apply_rope(x, cos, sin):
    half = x.shape[-1] // 2
    x1, x2 = x[..., :half], x[..., half:]
    c, s = cos.astype(x.dtype), sin.astype(x.dtype)
    return jnp.concatenate([x1 * c - x2 * s, x1 * s + x2 * c], axis=-1)

def pool_mixer(u, w_groups, scale):
    B, S, D = u.shape
    uf = u.astype(jnp.float32)
    c = jnp.cumsum(uf, axis=1)
    count = jnp.arange(1, S + 1, dtype=jnp.float32)[None, :, None]
    outs = []
    for g, w in enumerate(POOL_WINDOWS):
        sl = slice(g * POOL_GROUP, (g + 1) * POOL_GROUP)
        cg = c[..., sl]
        lag = jnp.pad(cg, ((0, 0), (w, 0), (0, 0)))[:, :S]
        mean = (cg - lag) / jnp.minimum(count, float(w))
        outs.append(mean - uf[..., sl])
    y = jnp.stack(outs, axis=2).astype(u.dtype)
    z = jnp.einsum('bsgc,gcd->bsgd', y, w_groups).reshape(B, S, D)
    return z * scale

def mla_shared_kv(h, kv_in_norm, w_dkv, ckv_norm, w_uk, w_uv, cos, sin):
    u = rmsnorm(h, kv_in_norm)
    kv_a = u @ w_dkv
    c_kv = rmsnorm(kv_a[..., :KV_LORA_RANK], ckv_norm)
    k_rope = apply_rope(kv_a[..., KV_LORA_RANK:], cos[None], sin[None])
    k_nope = jnp.einsum('bsr,rhd->bshd', c_kv, w_uk)
    v = jnp.einsum('bsr,rhd->bshd', c_kv, w_uv)
    return k_nope, k_rope, v

def mla_attention(u, q_lora_norm, w_dq, w_uq, w_o, k_nope, k_rope, v, cos, sin):
    B, S, _ = u.shape
    cq = rmsnorm(u @ w_dq, q_lora_norm)
    q = jnp.einsum('bsr,rhd->bshd', cq, w_uq)
    q_nope = q[..., :QK_NOPE_DIM]
    q_rope = apply_rope(q[..., QK_NOPE_DIM:], cos[None, :, None], sin[None, :, None])
    nblk = S // Q_BLOCK
    qn = q_nope.reshape(B, nblk, Q_BLOCK, N_HEADS, QK_NOPE_DIM).transpose(1, 0, 2, 3, 4)
    qr = q_rope.reshape(B, nblk, Q_BLOCK, N_HEADS, QK_ROPE_DIM).transpose(1, 0, 2, 3, 4)
    scale = QK_DIM ** -0.5
    key_pos = jnp.arange(S)

    def block(args):
        i, qn_b, qr_b = args
        s = (jnp.einsum('bqhd,bkhd->bhqk', qn_b, k_nope)
             + jnp.einsum('bqhr,bkr->bhqk', qr_b, k_rope))
        s = s.astype(jnp.float32) * scale
        q_pos = i * Q_BLOCK + jnp.arange(Q_BLOCK)
        mask = key_pos[None, :] <= q_pos[:, None]
        s = jnp.where(mask[None, None], s, -jnp.inf)
        p = jax.nn.softmax(s, axis=-1).astype(v.dtype)
        return jnp.einsum('bhqk,bkhd->bqhd', p, v)

    o = lax.map(block, (jnp.arange(nblk), qn, qr))
    o = o.transpose(1, 0, 2, 3, 4).reshape(B, S, N_HEADS * V_DIM)
    return o @ w_o

def first_inputs(seed: int = 0) -> dict:
    key = jax.random.key(seed)
    ks = jax.random.split(key, 32)
    f32 = jnp.float32

    def w(k, shape, fan_in):
        return jax.random.normal(k, shape, f32) * (fan_in ** -0.5)

    def gain(k, shape):
        return 1.0 + 0.02 * jax.random.normal(k, shape, f32)

    D, F, G, Dg = D_MODEL, D_FF, N_POOL_GROUPS, POOL_GROUP
    return {
        "x": jax.random.normal(ks[0], (BATCH, SEQ, D), f32),
        "ffn_pre_norm": gain(ks[1], (DEPTH, D)),
        "ffn_pre_wg": w(ks[2], (DEPTH, D, F), D),
        "ffn_pre_wu": w(ks[3], (DEPTH, D, F), D),
        "ffn_pre_wd": w(ks[4], (DEPTH, F, D), F),
        "mix_norm": gain(ks[5], (DEPTH, D)),
        "ffn_post_norm": gain(ks[6], (DEPTH, D)),
        "ffn_post_wg": w(ks[7], (DEPTH, D, F), D),
        "ffn_post_wu": w(ks[8], (DEPTH, D, F), D),
        "ffn_post_wd": w(ks[9], (DEPTH, F, D), F),
        "pool_w": w(ks[10], (N_A_LAYERS, G, Dg, Dg), Dg),
        "pool_scale": gain(ks[11], (N_A_LAYERS, D)),
        "kv_in_norm": gain(ks[12], (D,)),
        "w_dkv": w(ks[13], (D, KV_LORA_RANK + QK_ROPE_DIM), D),
        "ckv_norm": gain(ks[14], (KV_LORA_RANK,)),
        "w_uk": w(ks[15], (KV_LORA_RANK, N_HEADS, QK_NOPE_DIM), KV_LORA_RANK),
        "w_uv": w(ks[16], (KV_LORA_RANK, N_HEADS, V_DIM), KV_LORA_RANK),
        "q_lora_norm": gain(ks[17], (N_B_LAYERS, Q_LORA_RANK)),
        "w_dq": w(ks[18], (N_B_LAYERS, D, Q_LORA_RANK), D),
        "w_uq": w(ks[19], (N_B_LAYERS, Q_LORA_RANK, N_HEADS, QK_DIM), Q_LORA_RANK),
        "w_o": w(ks[20], (N_B_LAYERS, N_HEADS * V_DIM, D), N_HEADS * V_DIM),
        "final_norm": gain(ks[21], (D,)),
    }

def first_block(x, ffn_pre_norm, ffn_pre_wg, ffn_pre_wu, ffn_pre_wd, mix_norm,
              ffn_post_norm, ffn_post_wg, ffn_post_wu, ffn_post_wd,
              pool_w, pool_scale, kv_in_norm, w_dkv, ckv_norm, w_uk, w_uv,
              q_lora_norm, w_dq, w_uq, w_o, final_norm):
    S = x.shape[1]
    cos, sin = rope_tables(S)
    h = x
    k_nope = k_rope = v = None
    for l in range(DEPTH):
        h = h + 0.5 * swiglu(rmsnorm(h, ffn_pre_norm[l]), ffn_pre_wg[l], ffn_pre_wu[l], ffn_pre_wd[l])
        u = rmsnorm(h, mix_norm[l])
        if l < N_A_LAYERS:
            h = h + pool_mixer(u, pool_w[l], pool_scale[l])
        else:
            j = l - N_A_LAYERS
            h = h + mla_attention(u, q_lora_norm[j], w_dq[j], w_uq[j], w_o[j],
                                  k_nope, k_rope, v, cos, sin)
        h = h + 0.5 * swiglu(rmsnorm(h, ffn_post_norm[l]), ffn_post_wg[l], ffn_post_wu[l], ffn_post_wd[l])
        if l == N_A_LAYERS - 1:
            k_nope, k_rope, v = mla_shared_kv(h, kv_in_norm, w_dkv, ckv_norm, w_uk, w_uv, cos, sin)
    return rmsnorm(h, final_norm)


HEAD_DIM = 64
N_HEADS_2 = D_MODEL // HEAD_DIM
FOX_HEADS = N_HEADS_2 // 2
SWA_HEADS = N_HEADS_2 - FOX_HEADS
SWA_KV_HEADS = max(1, SWA_HEADS // 4)
SWA_WINDOW = 128
DSA_HEADS = N_HEADS_2
DSA_KV_HEADS = max(1, DSA_HEADS // 4)
IDX_HEADS = 8
IDX_DIM = 64
DSA_TOPK_MAX = 256
N_EXPERTS = 8
TOP_K = 2
D_FF_EXPERT = 1408
NORM_EPS = 1e-6
N_EVEN = (DEPTH + 1) // 2
N_ODD = DEPTH // 2

EVEN_SPLITS = (FOX_HEADS * HEAD_DIM, FOX_HEADS * HEAD_DIM, FOX_HEADS * HEAD_DIM, FOX_HEADS,
               SWA_HEADS * HEAD_DIM, SWA_KV_HEADS * HEAD_DIM, SWA_KV_HEADS * HEAD_DIM)
EVEN_IN = sum(EVEN_SPLITS)
ODD_SPLITS = (DSA_HEADS * HEAD_DIM, DSA_KV_HEADS * HEAD_DIM, DSA_KV_HEADS * HEAD_DIM,
              IDX_HEADS * IDX_DIM, IDX_DIM, IDX_HEADS)
ODD_IN = sum(ODD_SPLITS)


def _split(t, sizes):
    return jnp.split(t, np.cumsum(sizes)[:-1].tolist(), axis=-1)

def rms_norm(x, g):
    xf = x.astype(jnp.float32)
    y = xf * lax.rsqrt(jnp.mean(xf * xf, axis=-1, keepdims=True) + NORM_EPS)
    return (y * g.astype(jnp.float32)).astype(x.dtype)

def ada_modulation(c, w, b):
    mod = jax.nn.silu(c) @ w + b
    return jnp.split(mod[:, None, :], 6, axis=-1)

def rope_tables_2(positions, dim):
    half = dim // 2
    inv_freq = ROPE_THETA ** (-jnp.arange(half, dtype=jnp.float32) / half)
    ang = positions.astype(jnp.float32)[..., None] * inv_freq
    return jnp.cos(ang)[:, :, None, :], jnp.sin(ang)[:, :, None, :]

def apply_rope_2(t, cos, sin):
    half = t.shape[-1] // 2
    tf = t.astype(jnp.float32)
    t1, t2 = tf[..., :half], tf[..., half:]
    return jnp.concatenate([t1 * cos - t2 * sin, t2 * cos + t1 * sin], axis=-1).astype(t.dtype)

def swiglu_2(h, w_gate, w_up, w_down):
    return (jax.nn.silu(h @ w_gate) * (h @ w_up)) @ w_down

def forgetting_attention(q, k, v, log_f):
    B, S, H, D = q.shape
    cum = jnp.cumsum(log_f.astype(jnp.float32), axis=1).transpose(0, 2, 1)
    kpos = jnp.arange(S)
    scale = D ** -0.5

    def block(i):
        start = i * Q_BLOCK
        qi = lax.dynamic_slice_in_dim(q, start, Q_BLOCK, axis=1)
        ci = lax.dynamic_slice_in_dim(cum, start, Q_BLOCK, axis=2)
        s = jnp.einsum('bqhd,bkhd->bhqk', qi, k, preferred_element_type=jnp.float32) * scale
        s = s + ci[..., :, None] - cum[..., None, :]
        qpos = start + jnp.arange(Q_BLOCK)
        s = jnp.where(kpos[None, :] <= qpos[:, None], s, -jnp.inf)
        p = jax.nn.softmax(s, axis=-1)
        return jnp.einsum('bhqk,bkhd->bqhd', p.astype(v.dtype), v)

    out = lax.map(block, jnp.arange(S // Q_BLOCK))
    return jnp.moveaxis(out, 0, 1).reshape(B, S, H, D)

def sliding_window_sink_attention(q, k, v, sinks):
    B, S, H, D = q.shape
    KVH = k.shape[2]
    G = H // KVH
    W = SWA_WINDOW
    nb = S // W
    qb = q.reshape(B, nb, W, KVH, G, D)

    def band_keys(t):
        tb = t.reshape(B, nb, W, KVH, D)
        prev = jnp.concatenate([jnp.zeros_like(tb[:, :1]), tb[:, :-1]], axis=1)
        return jnp.concatenate([prev, tb], axis=2)

    kk, vv = band_keys(k), band_keys(v)
    s = jnp.einsum('bnqhgd,bnshd->bnhgqs', qb, kk, preferred_element_type=jnp.float32) * D ** -0.5
    rel = (jnp.arange(W)[:, None] + W) - jnp.arange(2 * W)[None, :]
    band = (rel >= 0) & (rel < W)
    not_pad = (jnp.arange(nb)[:, None, None] > 0) | (jnp.arange(2 * W) >= W)[None, None, :]
    valid = band[None] & not_pad
    s = jnp.where(valid[None, :, None, None], s, -jnp.inf)
    sink = sinks.astype(jnp.float32).reshape(KVH, G)[None, None, :, :, None, None]
    m = jnp.maximum(jnp.max(s, axis=-1, keepdims=True), sink)
    e = jnp.exp(s - m)
    p = e / (jnp.sum(e, axis=-1, keepdims=True) + jnp.exp(sink - m))
    out = jnp.einsum('bnhgqs,bnshd->bnqhgd', p.astype(v.dtype), vv)
    return out.reshape(B, S, H, D)

def dsa_attention(q, k, v, iq, ik, iw):
    B, S, H, D = q.shape
    KVH = k.shape[2]
    G = H // KVH
    topk = min(DSA_TOPK_MAX, S // 4)
    kpos = jnp.arange(S)
    scale = D ** -0.5
    gather = jax.vmap(lambda tb, ib: tb[ib])

    def block(i):
        start = i * Q_BLOCK
        qi = lax.dynamic_slice_in_dim(q, start, Q_BLOCK, axis=1).reshape(B, Q_BLOCK, KVH, G, D)
        iqi = lax.dynamic_slice_in_dim(iq, start, Q_BLOCK, axis=1)
        iwi = lax.dynamic_slice_in_dim(iw, start, Q_BLOCK, axis=1).astype(jnp.float32)
        qpos = start + jnp.arange(Q_BLOCK)
        logits = jnp.einsum('bqhd,bsd->bqhs', iqi, ik, preferred_element_type=jnp.float32)
        score = jnp.einsum('bqh,bqhs->bqs', iwi, jax.nn.relu(logits))
        score = jnp.where((kpos[None, :] <= qpos[:, None])[None], score, -jnp.inf)
        _, idx = lax.top_k(score, topk)
        sel_valid = idx <= qpos[None, :, None]
        ks = gather(k, idx)
        vs = gather(v, idx)
        s = jnp.einsum('bqhgd,bqthd->bhgqt', qi, ks, preferred_element_type=jnp.float32) * scale
        s = jnp.where(sel_valid[:, None, None], s, -jnp.inf)
        p = jax.nn.softmax(s, axis=-1)
        o = jnp.einsum('bhgqt,bqthd->bqhgd', p.astype(v.dtype), vs)
        return o.reshape(B, Q_BLOCK, H, D)

    out = lax.map(block, jnp.arange(S // Q_BLOCK))
    return jnp.moveaxis(out, 0, 1).reshape(B, S, H, D)

def moe_swiglu(h, router_w, router_b, w_gate, w_up, w_down):
    B, S, Dm = h.shape
    t = h.reshape(B * S, Dm)
    logits = (t @ router_w).astype(jnp.float32) + router_b.astype(jnp.float32)
    top_vals, top_idx = lax.top_k(logits, TOP_K)
    gates = jax.nn.softmax(top_vals, axis=-1)
    combine = jnp.sum(jax.nn.one_hot(top_idx, N_EXPERTS, dtype=jnp.float32) * gates[..., None], axis=1)
    combine = combine.astype(h.dtype)
    out = jnp.zeros_like(t)
    for e in range(N_EXPERTS):
        out = out + combine[:, e:e + 1] * swiglu_2(t, w_gate[e], w_up[e], w_down[e])
    return out.reshape(B, S, Dm)

def even_layer(x, c, cos, sin, ada_w, ada_b, norm_mix, norm_ffn, w_in, forget_b, sinks, w_out,
               ffn_gate, ffn_up, ffn_down):
    B, S, _ = x.shape
    sh_m, sc_m, g_m, sh_f, sc_f, g_f = ada_modulation(c, ada_w, ada_b)
    h = rms_norm(x, norm_mix) * (1 + sc_m) + sh_m
    fq, fk, fv, fgl, sq, sk, sv = _split(h @ w_in, EVEN_SPLITS)
    heads = lambda t, n: t.reshape(B, S, n, HEAD_DIM)
    log_f = jax.nn.log_sigmoid((fgl + forget_b).astype(jnp.float32))
    o_fox = forgetting_attention(heads(fq, FOX_HEADS), heads(fk, FOX_HEADS), heads(fv, FOX_HEADS), log_f)
    o_swa = sliding_window_sink_attention(apply_rope_2(heads(sq, SWA_HEADS), cos, sin),
                                          apply_rope_2(heads(sk, SWA_KV_HEADS), cos, sin),
                                          heads(sv, SWA_KV_HEADS), sinks)
    mix = jnp.concatenate([o_fox.reshape(B, S, -1), o_swa.reshape(B, S, -1)], axis=-1) @ w_out
    x = x + g_m * mix
    h = rms_norm(x, norm_ffn) * (1 + sc_f) + sh_f
    return x + g_f * swiglu_2(h, ffn_gate, ffn_up, ffn_down)

def odd_layer(x, c, cos, sin, ada_w, ada_b, norm_mix, norm_ffn, w_in, w_out,
              router_w, router_b, exp_gate, exp_up, exp_down):
    B, S, _ = x.shape
    sh_m, sc_m, g_m, sh_f, sc_f, g_f = ada_modulation(c, ada_w, ada_b)
    h = rms_norm(x, norm_mix) * (1 + sc_m) + sh_m
    q, k, v, iq, ik, iw = _split(h @ w_in, ODD_SPLITS)
    q = apply_rope_2(q.reshape(B, S, DSA_HEADS, HEAD_DIM), cos, sin)
    k = apply_rope_2(k.reshape(B, S, DSA_KV_HEADS, HEAD_DIM), cos, sin)
    v = v.reshape(B, S, DSA_KV_HEADS, HEAD_DIM)
    iq = apply_rope_2(iq.reshape(B, S, IDX_HEADS, IDX_DIM), cos, sin)
    ik = apply_rope_2(ik.reshape(B, S, 1, IDX_DIM), cos, sin)[:, :, 0]
    iw = iw * (IDX_HEADS ** -0.5 * IDX_DIM ** -0.5)
    o = dsa_attention(q, k, v, iq, ik, iw)
    x = x + g_m * (o.reshape(B, S, -1) @ w_out)
    h = rms_norm(x, norm_ffn) * (1 + sc_f) + sh_f
    return x + g_f * moe_swiglu(h, router_w, router_b, exp_gate, exp_up, exp_down)

def second_inputs(seed: int = 0) -> dict:
    key = jax.random.key(seed)
    ks = iter(jax.random.split(key, 40))
    D = D_MODEL

    def nrm(shape, s):
        return jax.random.normal(next(ks), shape, jnp.float32) * s

    x = nrm((BATCH, SEQ, D), 1.0)
    c = nrm((BATCH, D), 1.0)
    offset = jax.random.randint(next(ks), (BATCH, 1), 0, 4096, dtype=jnp.int32)
    positions = offset + jnp.arange(SEQ, dtype=jnp.int32)[None, :]
    return {
        'x': x, 'c': c, 'positions': positions,
        'e_ada_w': nrm((N_EVEN, D, 6 * D), 0.5 * D ** -0.5),
        'e_ada_b': nrm((N_EVEN, 6 * D), 0.02),
        'e_norm_mix': 1.0 + nrm((N_EVEN, D), 0.05),
        'e_norm_ffn': 1.0 + nrm((N_EVEN, D), 0.05),
        'e_w_in': nrm((N_EVEN, D, EVEN_IN), D ** -0.5),
        'e_forget_b': 3.0 + nrm((N_EVEN, FOX_HEADS), 1.0),
        'e_sinks': nrm((N_EVEN, SWA_HEADS), 1.0),
        'e_w_out': nrm((N_EVEN, D, D), D ** -0.5),
        'e_ffn_gate': nrm((N_EVEN, D, D_FF), D ** -0.5),
        'e_ffn_up': nrm((N_EVEN, D, D_FF), D ** -0.5),
        'e_ffn_down': nrm((N_EVEN, D_FF, D), D_FF ** -0.5),
        'o_ada_w': nrm((N_ODD, D, 6 * D), 0.5 * D ** -0.5),
        'o_ada_b': nrm((N_ODD, 6 * D), 0.02),
        'o_norm_mix': 1.0 + nrm((N_ODD, D), 0.05),
        'o_norm_ffn': 1.0 + nrm((N_ODD, D), 0.05),
        'o_w_in': nrm((N_ODD, D, ODD_IN), D ** -0.5),
        'o_w_out': nrm((N_ODD, D, D), D ** -0.5),
        'o_router_w': nrm((N_ODD, D, N_EXPERTS), D ** -0.5),
        'o_router_b': nrm((N_ODD, N_EXPERTS), 0.01),
        'o_exp_gate': nrm((N_ODD, N_EXPERTS, D, D_FF_EXPERT), D ** -0.5),
        'o_exp_up': nrm((N_ODD, N_EXPERTS, D, D_FF_EXPERT), D ** -0.5),
        'o_exp_down': nrm((N_ODD, N_EXPERTS, D_FF_EXPERT, D), D_FF_EXPERT ** -0.5),
        'final_norm': 1.0 + nrm((D,), 0.05),
    }

def second_block(x, c, positions,
              e_ada_w, e_ada_b, e_norm_mix, e_norm_ffn, e_w_in, e_forget_b, e_sinks, e_w_out,
              e_ffn_gate, e_ffn_up, e_ffn_down,
              o_ada_w, o_ada_b, o_norm_mix, o_norm_ffn, o_w_in, o_w_out,
              o_router_w, o_router_b, o_exp_gate, o_exp_up, o_exp_down,
              final_norm):
    cos, sin = rope_tables_2(positions, HEAD_DIM)
    for layer in range(DEPTH):
        i = layer // 2
        if layer % 2 == 0:
            x = even_layer(x, c, cos, sin, e_ada_w[i], e_ada_b[i], e_norm_mix[i], e_norm_ffn[i],
                           e_w_in[i], e_forget_b[i], e_sinks[i], e_w_out[i],
                           e_ffn_gate[i], e_ffn_up[i], e_ffn_down[i])
        else:
            x = odd_layer(x, c, cos, sin, o_ada_w[i], o_ada_b[i], o_norm_mix[i], o_norm_ffn[i],
                          o_w_in[i], o_w_out[i], o_router_w[i], o_router_b[i],
                          o_exp_gate[i], o_exp_up[i], o_exp_down[i])
    return rms_norm(x, final_norm)


def setup_inputs(seed=0):
    out = dict(first_inputs(seed))
    for name, value in second_inputs(seed + 1).items():
        if name != "x":
            out[name + "_2"] = value
    return out


def reference(
    x, ffn_pre_norm, ffn_pre_wg, ffn_pre_wu, ffn_pre_wd, mix_norm, ffn_post_norm, ffn_post_wg,
    ffn_post_wu, ffn_post_wd, pool_w, pool_scale, kv_in_norm, w_dkv, ckv_norm, w_uk, w_uv,
    q_lora_norm, w_dq, w_uq, w_o, final_norm, c_2, positions_2, e_ada_w_2, e_ada_b_2,
    e_norm_mix_2, e_norm_ffn_2, e_w_in_2, e_forget_b_2, e_sinks_2, e_w_out_2, e_ffn_gate_2,
    e_ffn_up_2, e_ffn_down_2, o_ada_w_2, o_ada_b_2, o_norm_mix_2, o_norm_ffn_2, o_w_in_2,
    o_w_out_2, o_router_w_2, o_router_b_2, o_exp_gate_2, o_exp_up_2, o_exp_down_2, final_norm_2,
):
    x = first_block(
        x, ffn_pre_norm, ffn_pre_wg, ffn_pre_wu, ffn_pre_wd, mix_norm, ffn_post_norm,
        ffn_post_wg, ffn_post_wu, ffn_post_wd, pool_w, pool_scale, kv_in_norm, w_dkv, ckv_norm,
        w_uk, w_uv, q_lora_norm, w_dq, w_uq, w_o, final_norm,
    )
    return second_block(
        x, c_2, positions_2, e_ada_w_2, e_ada_b_2, e_norm_mix_2, e_norm_ffn_2, e_w_in_2,
        e_forget_b_2, e_sinks_2, e_w_out_2, e_ffn_gate_2, e_ffn_up_2, e_ffn_down_2, o_ada_w_2,
        o_ada_b_2, o_norm_mix_2, o_norm_ffn_2, o_w_in_2, o_w_out_2, o_router_w_2, o_router_b_2,
        o_exp_gate_2, o_exp_up_2, o_exp_down_2, final_norm_2,
    )


_drawn_inputs = setup_inputs


def setup_inputs(seed=0):
    import zlib

    import numpy as np

    out = dict(_drawn_inputs(seed))
    spreads = {}
    factors = {'ffn_pre_norm': 3.388,
     'ffn_post_norm': 3.902,
     'pool_scale': 2.936,
     'kv_in_norm': 7.463,
     'ckv_norm': 7.177,
     'q_lora_norm': 8.0,
     'e_norm_mix_2': 4.246,
     'e_norm_ffn_2': 2.726,
     'e_sinks_2': 4.407,
     'o_norm_mix_2': 2.738,
     'o_norm_ffn_2': 2.776,
     'o_router_b_2': 7.553}
    for name, (base, spread) in spreads.items():
        noise = np.random.default_rng([zlib.crc32(name.encode()), seed]).standard_normal(out[name].shape)
        drawn = base * np.exp(spread * noise) if base else spread * noise
        out[name] = __import__('jax').numpy.asarray(drawn.astype(out[name].dtype))
    for name, factor in factors.items():
        out[name] = (out[name] * factor).astype(out[name].dtype)
    return out
```

```python
from contextlib import ExitStack, contextmanager

import numpy as np

import concourse.bass as bass
from concourse import mybir

F32 = mybir.dt.float32
F32R = mybir.dt.float32r
I32 = mybir.dt.int32
U32 = mybir.dt.uint32
ALU = mybir.AluOpType
ACT = mybir.ActivationFunctionType
AX_X = mybir.AxisListType.X

P = 128
S = 256
TT = S // P
D = 1024
DC = D // P
F = 2816
BW = 256
FB = F // BW
EPS = 1e-6
NEG = -1e30
BLOCK = DC * BW
RING = 3
HEADS_A, NOPE, ROPE, VD = 16, 128, 64, 128
QL, KVL = 256, 128
GH = 4
HD = 64
E, TOPE, FE = 8, 2, 1408
IH = 8
TOPK = min(256, S // 4)
FOXH = 8
N_SMALL = 7
ROUND = 1.5 * 2.0 ** 23
TURN = [6.28125]
TURN.append(float(np.round((2.0 * np.pi - TURN[0]) * 2.0 ** 22) / 2.0 ** 22))
TURN.append(2.0 * np.pi - TURN[0] - TURN[1])
HALF_TURN = 3.1415925
TAKEN = -3e38

Q_PARTS = ((0, 3), (3, 6), (6, 8))
UQ = GH * (NOPE + ROPE)
UQ_PARTS = (UQ, UQ // 2, UQ // 2)
Q_TILES = ((0, P), (P, P + S))
G_MLA, G_FOX, G_WIN, G_DSA = 1, 5, 7, 9

STREAM = {}
_at = 0
for _name, _n in [("ffn0", 3 * FB), ("pool", 1), ("ffn1", 3 * FB), ("dkv", 1), ("ffn2", 3 * FB),
                  ("dq", 1), ("uk", 1), ("uv", 1), ("uq", 12), ("wo", 8), ("ffn3", 3 * FB),
                  ("fk", 2), ("fv", 2), ("fq", 6), ("skv", 1), ("sq", 6), ("ewo", 4), ("ffn4", 3 * FB),
                  ("iq", 2), ("ikw", 1), ("dk", 1), ("dv", 1), ("dsq", 12), ("owo", 4), ("moe", E * 18)]:
    STREAM[_name] = _at
    _at += _n

VEC = {}
_at = 0
for _name, _n in [("ffn_pre", 16), ("mix", 16), ("ffn_post", 16), ("pool_scale", 8), ("kv_in", 8),
                  ("final1", 8), ("e_mix", 8), ("e_ffn", 8), ("o_mix", 8), ("o_ffn", 8), ("final2", 8),
                  ("c", 8), ("ckv", 1), ("q_lora", 2)]:
    VEC[_name] = (_at, _n)
    _at += _n
NV = _at
VEC_SRC = {"ffn_pre": "ffn_pre_norm", "mix": "mix_norm", "ffn_post": "ffn_post_norm", "pool_scale": "pool_scale",
           "kv_in": "kv_in_norm", "final1": "final_norm", "e_mix": "e_norm_mix_2", "e_ffn": "e_norm_ffn_2",
           "o_mix": "o_norm_mix_2", "o_ffn": "o_norm_ffn_2", "final2": "final_norm_2", "c": "c_2",
           "ckv": "ckv_norm", "q_lora": "q_lora_norm"}
N_VEC_DMAS = len(VEC_SRC) + 2
NA = 96

CONST = {}
_at = 0
for _name, _n in [("ident", P), ("ones", P), ("rot", P), ("swap", P), ("causal", P + S), ("window", P + S),
                  ("cos", S), ("sin", S), ("neg_ident", 4), ("ident4", 4), ("inv_freq", 1),
                  ("numbers", E)]:
    CONST[_name] = (_at, _n)
    _at += _n
NC = _at


def constants():
    t = np.zeros((P, NC), np.float32)

    def put(name, value):
        a, n = CONST[name]
        t[:, a:a + n] = value

    row, col = np.arange(P)[:, None], np.arange(P)[None, :]
    put("ident", np.eye(P))
    put("ones", 1.0)
    half = ROPE // 2
    put("rot", np.where((col % ROPE < half) & (row == col + half), -1.0, 0.0)
        + np.where((col % ROPE >= half) & (row == col - half), 1.0, 0.0))
    put("swap", row == (col + HD) % P)
    put("numbers", np.arange(E)[None, :])
    key = np.arange(S)[None, :]
    first = np.where(col <= row, 0.0, NEG)
    put("causal", np.concatenate([first, np.where(key <= row + P, 0.0, NEG)], 1))
    put("window", np.concatenate([first, np.where((key <= row + P) & (key > row), 0.0, NEG)], 1))
    dim = np.arange(0, ROPE, 2, dtype=np.float32) / np.float32(ROPE)
    inv = (np.float32(10000.0) ** -dim).astype(np.float32)
    ang = (inv[np.arange(P) % half][:, None] * key.astype(np.float32)).astype(np.float32)
    put("cos", np.cos(ang.astype(np.float64)))
    put("sin", np.sin(ang.astype(np.float64)))
    put("neg_ident", -np.eye(P)[:, :4])
    put("ident4", np.eye(P)[:, :4])
    put("inv_freq", inv[np.arange(P) % half][:, None])
    return t


def window_counts():
    key = np.arange(S)[None, :]
    rows = np.concatenate([1.0 / np.minimum(key + 1, w) for w in (2, 4, 8, 16)], 1)
    return np.broadcast_to(rows, (P, 4 * S)).astype(np.float32)


class Chain:

    def __init__(self, eng, sem):
        self.eng, self.sem, self.n, self.lap, self.per = eng, sem, 0, None, 0

    def link(self, ins):
        ins.then_inc(self.sem, 1)
        self.n += 1
        self.eng.wait_ge(self.sem, self.n if self.lap is None else self.lap * self.per + self.n)

    @contextmanager
    def laps(self, lap, count, per):
        start, self.lap, self.per = self.n, lap, per
        yield
        assert self.n - start == per, (self.n - start, per)
        self.n, self.lap = start + per * count, None


def hold(eng, sem, value):
    if not isinstance(value, int) or value > 0:
        eng.wait_ge(sem, value)


def wide(ap, n):
    return ap.unsqueeze(1).broadcast_to([ap.shape[0], n, ap.shape[1]])


def whole(n=BLOCK):
    return [(lambda w: w[:, 0:n], lambda w: w[:, 0:n])]


def heads_apart(h):
    def src(w):
        return w[:, 0:h * (NOPE + ROPE)].rearrange("p (h n) -> p h n", h=h)

    return [(lambda w: src(w)[:, :, 0:NOPE], lambda w: w[:, 0:h * NOPE].rearrange("p (h n) -> p h n", h=h)),
            (lambda w: src(w)[:, :, NOPE:],
             lambda w: w[:, h * NOPE:h * (NOPE + ROPE)].rearrange("p (h n) -> p h n", h=h))]


def two_blocks_kernel(nc, a, out):
    ctx = ExitStack()
    with ctx:
        def sb(name, shape, dt=F32, into=ctx):
            return into.enter_context(nc.sbuf_tensor(name, shape, dt))

        def sem(name):
            return ctx.enter_context(nc.semaphore(name))

        C = sb("consts", [P, NC])
        VT = sb("vectors", [P, NV])
        ABT = sb("ada_bias", [P, NA])
        X = sb("residual", [P, DC, S])
        UH = sb("u_high", [P, DC, S], F32R)
        UL = sb("u_low", [P, DC, S], F32R)
        T = sb("scratch", [P, DC, S])
        RAW = [sb(f"raw{s}", [P, BLOCK]) for s in range(RING)]
        WH = [sb(f"w_high{s}", [P, BLOCK], F32R) for s in range(RING)]
        WL = [sb(f"w_low{s}", [P, BLOCK], F32R) for s in range(RING)]
        RAWA = sb("raw_ada", [P, BLOCK])
        R = sb("inv_rms", [P, S])
        RV = sb("inv_var", [P, S])
        SS = sb("square_sums", [P, 2 * S])
        MOD = sb("modulation", [P, NA])
        CS = sb("silu_c", [P, DC])
        CKH = sb("ckv_high", [P, S], F32R)
        CKL = sb("ckv_low", [P, S], F32R)
        KRZ = sb("k_rope_padded", [P, 2, S])
        COSP = sb("position_cos", [P, S])
        SINP = sb("position_sin", [P, S])
        POSI = sb("positions", [P, S], I32)
        FG = sb("forget_weights", [P, DC, FOXH])
        RW = sb("router_weights", [P, DC, E])
        FB4 = sb("forget_bias", [4, 2])
        SINK = sb("sinks", [P, 2, FOXH])
        RB = sb("router_bias", [P, E])
        ADA = sb("ada_scale", [P, DC])

        def const(name):
            at, n = CONST[name]
            return C[:, at:at + n]

        def vec(name, k=0, n=DC):
            at = VEC[name][0] + k
            return VT[:, at:at + n]

        with ExitStack() as stage:
            XIN = sb("x_in", [P, TT, D], into=stage)
            VR = sb("vector_rows", [P, P], into=stage)
            AR = sb("ada_bias_rows", [P, P], into=stage)
        with ExitStack() as stage:
            GS = sb("gate_scaled", [P, 2 * S], into=stage)
            US = sb("up_scaled", [P, 2 * S], into=stage)
            SG = sb("gate_silu", [P, 2 * S], into=stage)
            HF = sb("hidden", [P, 2, S], into=stage)
            HH = sb("hidden_high", [P, 4, S], F32R, into=stage)
            HL = sb("hidden_low", [P, 4, S], F32R, into=stage)
        with ExitStack() as stage:
            PB = [sb(f"window_sum{k}", [P, 2, 8 + S], into=stage) for k in range(2)]
            PY = sb("pooled", [P, 2, S], into=stage)
            sb("beyond_the_ffn", [P, 3 * BLOCK], into=stage)
            INVC = sb("inv_count", [P, 4, S], into=stage)
        with ExitStack() as stage:
            KN = sb("k_nope", [P, HEADS_A, S], into=stage)
            V = sb("v_latent", [P, TT, HEADS_A * VD], into=stage)
            OH = sb("o_high", [P, HEADS_A, S], F32R, into=stage)
            OL = sb("o_low", [P, HEADS_A, S], F32R, into=stage)
            PR = [sb(f"probs{k}", [P, P + S], into=stage) for k in range(GH)]
            PT = [sb(f"probs_turned{k}", [P, P + S], into=stage) for k in range(2)]
            SM = sb("softmax_small", [P, GH, 8], into=stage)
        with ExitStack() as stage:
            W = sb("index_scores", [P, P + S], into=stage)
            SEL = sb("selected", [P, P + S], into=stage)
            RL = [sb(f"relu{k}", [P, P + S], into=stage) for k in range(2)]
            IQ = sb("index_queries", [P, 4, S], into=stage)
            IWT = sb("index_weights", [P, TT, IH], into=stage)
            M8 = sb("largest", [P, 8], into=stage)
        with ExitStack() as stage:
            LX = sb("forget_logits", [4, 2, S], into=stage)
            LM = sb("forget_softplus", [4, 2, S], into=stage)
            CIT = sb("forget_of_query", [P, 2, TT, GH], into=stage)
            ANG = [sb(f"angle{k}", [P, S], into=stage) for k in range(2)]
        with ExitStack() as stage:
            sb("ffn_part", [P, HEADS_A * S], into=stage)
            KZ = sb("keys_padded", [P, 8, S], into=stage)
            V2 = sb("values", [P, TT, 512], into=stage)
            CUM = sb("forget_sums", [4, 2, S], into=stage)
            IKZ = sb("index_keys_padded", [P, 2, S], into=stage)
        with ExitStack() as stage:
            LG = sb("router_logits", [P, TT, E], into=stage)
            TOP = sb("router_top", [P, TT, 8], into=stage)
            TOPI = sb("router_top_index", [P, TT, 8], U32, into=stage)
            TOPF = sb("router_top_number", [P, TT, 8], into=stage)
            GATE = sb("router_gates", [P, TT, 4], into=stage)
            ONE1 = sb("router_first", [P, TT, E], into=stage)
            COMBT = sb("router_combine", [P, TT, E], into=stage)
        VSD = RAWA[:, 0:TT * P].rearrange("p (t n) -> p t n", t=TT)
        QCH, QCL = UH[:, 0:2, :], UL[:, 0:2, :]
        VS = RAWA[:, 0:TT * GH * VD].rearrange("p (t n) -> p t n", t=TT)

        ACC = ctx.enter_context(nc.psum_tensor("acc", [P, 4 * 512], F32))
        GB = ctx.enter_context(nc.psum_tensor("gate_bank", [P, 512], F32))
        UB = ctx.enter_context(nc.psum_tensor("up_bank", [P, 512], F32))
        MB = ctx.enter_context(nc.psum_tensor("misc_bank", [P, 512], F32))
        SB = ctx.enter_context(nc.psum_tensor("stats_bank", [P, 512], F32))

        in_const, in_x, in_vec, in_inv = sem("in_const"), sem("in_x"), sem("in_vec"), sem("in_inv")
        raw_landed = [sem(f"raw_landed{s}") for s in range(RING)]
        hi_ready, lo_ready, w_used = sem("hi_ready"), sem("lo_ready"), sem("w_used")
        ada_landed, ada_used, ada_read = sem("ada_landed"), sem("ada_used"), sem("ada_read")
        x_ready = sem("x_ready")
        u_hi, u_lo = sem("u_hi"), sem("u_lo")
        sq_done, ss_done, stats_done = sem("sq_done"), sem("ss_done"), sem("stats_done")
        var_inv, r_done = sem("var_inv"), sem("r_done")
        g_free, u_free, silu_done = sem("g_free"), sem("u_free"), sem("silu_done")
        h_done, h_hi, h_lo = sem("h_done"), sem("h_hi"), sem("h_lo")
        acc_full = sem("acc_full")
        turned, vec_ready, c_ready = sem("turned"), sem("vec_ready"), sem("c_ready")
        dve_chain, act_chain = sem("dve_chain"), sem("act_chain")
        padded, pooled, zeroed = sem("padded"), sem("pooled"), sem("zeroed")
        kv_mm, kv_vec, kv_act = sem("kv_mm"), sem("kv_vec"), sem("kv_act")
        q_mm, q_vec, q_act = sem("q_mm"), sem("q_vec"), sem("q_act")
        k_full, k_out, v_full, v_out = sem("k_full"), sem("k_out"), sem("v_full"), sem("v_out")
        at_q, at_rot, at_qr = sem("at_q"), sem("at_rot"), sem("at_qr")
        at_score, at_max, at_exp, at_prob = sem("at_score"), sem("at_max"), sem("at_exp"), sem("at_prob")
        at_turned, at_pt, at_pv, at_oh, at_ol = (
            sem("at_turned"), sem("at_pt"), sem("at_pv"), sem("at_oh"), sem("at_ol"))
        v_staged = sem("v_staged")
        out_turned, out_copied, out_stored = sem("out_turned"), sem("out_copied"), sem("out_stored")
        in_small, trig_vec, trig_act = sem("in_small"), sem("trig_vec"), sem("trig_act")
        normed = sem("normed")
        fg_mm, fg_vec, fg_act = sem("fg_mm"), sem("fg_vec"), sem("fg_act")
        key_mm, key_vec, pads = sem("key_mm"), sem("key_vec"), sem("pads")
        ix_mm, ix_act, ix_vec = sem("ix_mm"), sem("ix_act"), sem("ix_vec")
        rt_mm, rt_vec, rt_act = sem("rt_mm"), sem("rt_vec"), sem("rt_act")

        block = ctx.enter_context(nc.Block())

        @block.sync
        def _(sp):
            def load(c, src, i=0):
                if not isinstance(i, int) or c >= RING:
                    sp.wait_ge(lo_ready, i * 3 + (c - RING + 1))
                shape = src.shape
                n = int(np.prod([int(k) for k in shape[1:]]))
                dst = RAW[c % RING][:, 0:n]
                if len(shape) == 3:
                    dst = dst.rearrange("p (k n) -> p k n", k=shape[1])
                sp.dma_start(dst, src).then_inc(raw_landed[c % RING], 16)

            def cols(w, i, n=BW, at=0):
                return w.rearrange("(k p) n -> p k n", p=P)[:, :, bass.ds(i * n + at, n)]

            def rows(w, i):
                return w.rearrange("(k p) n -> p k n", p=P)[:, bass.ds(i * 2, 2), :]

            def ffn(name, wg, wu, wd):
                b0 = STREAM[name]
                load(b0, cols(wg, 0))
                load(b0 + 1, cols(wu, 0))
                with sp.Fori(1, FB) as i:
                    load(b0 - 1, cols(wg, i), i)
                    load(b0, cols(wu, i), i)
                    load(b0 + 1, rows(wd, i - 1), i)
                load(b0 + 3 * FB - 1, rows(wd, FB - 1))

            def q_groups(name, w, n, at):
                with sp.Fori(0, n) as g:
                    for part, (k0, k1) in enumerate(Q_PARTS):
                        load(STREAM[name] + part, cols(w, g, at=at)[:, k0:k1, :], g)

            sp.dma_start(C[:, :], a["consts"]).then_inc(in_const, 16)
            sp.dma_start(XIN[:, :, :], a["x"][0].rearrange("(t p) n -> p t n", p=P)).then_inc(in_x, 16)
            ffn("ffn0", a["ffn_pre_wg"][0], a["ffn_pre_wu"][0], a["ffn_pre_wd"][0])
            load(STREAM["pool"], a["pool_w"][0].rearrange("g c n -> (g c) n").rearrange("(k p) n -> p k n", p=P))
            ffn("ffn1", a["ffn_post_wg"][0], a["ffn_post_wu"][0], a["ffn_post_wd"][0])
            load(STREAM["dkv"], cols(a["w_dkv"], 0, KVL + ROPE))
            ffn("ffn2", a["ffn_pre_wg"][1], a["ffn_pre_wu"][1], a["ffn_pre_wd"][1])
            load(STREAM["dq"], cols(a["w_dq"][0], 0))
            load(STREAM["uk"], a["w_uk"].rearrange("r h d -> r (h d)"))
            load(STREAM["uv"], a["w_uv"].rearrange("r h d -> r (h d)"))
            wq = a["w_uq"][0].rearrange("(k p) h d -> p k (h d)", p=P)
            with sp.Fori(0, HEADS_A // GH) as g:
                load(STREAM["uq"], wq[:, 0, bass.ds(g * UQ, UQ)], g)
                load(STREAM["uq"] + 1, wq[:, 1, bass.ds(g * UQ, UQ // 2)], g)
                load(STREAM["uq"] + 2, wq[:, 1, bass.ds(g * UQ + UQ // 2, UQ // 2)], g)
            b = STREAM["wo"]
            load(b, rows(a["w_o"][0], 0))
            with sp.Fori(0, 2) as i:
                for j in range(3):
                    load(b + 1 + j, rows(a["w_o"][0], i * 3 + (1 + j)), i)
            load(b + 7, rows(a["w_o"][0], 7))
            ffn("ffn3", a["ffn_post_wg"][1], a["ffn_post_wu"][1], a["ffn_post_wd"][1])
            w_in = a["e_w_in_2"][0]
            for j in range(2):
                load(STREAM["fk"] + j, cols(w_in, j, at=512))
            for j in range(2):
                load(STREAM["fv"] + j, cols(w_in, j, at=1024))
            q_groups("fq", w_in, 2, 0)
            load(STREAM["skv"], cols(w_in, 0, at=2056))
            q_groups("sq", w_in, 2, 1544)
            for j in range(4):
                load(STREAM["ewo"] + j, rows(a["e_w_out_2"][0], j))
            ffn("ffn4", a["e_ffn_gate_2"][0], a["e_ffn_up_2"][0], a["e_ffn_down_2"][0])
            w_in = a["o_w_in_2"][0]
            for j in range(2):
                load(STREAM["iq"] + j, cols(w_in, j, at=1536))
            load(STREAM["ikw"], cols(w_in, 0, HD + IH, at=2048))
            load(STREAM["dk"], cols(w_in, 0, at=1024))
            load(STREAM["dv"], cols(w_in, 0, at=1280))
            q_groups("dsq", w_in, 4, 0)
            for j in range(4):
                load(STREAM["owo"] + j, rows(a["o_w_out_2"][0], j))

            wg, wu = (a[k][0].rearrange("e (k p) n -> p (e k) n", p=P) for k in ("o_exp_gate_2", "o_exp_up_2"))
            wd = a["o_exp_down_2"][0].rearrange("e (c p) n -> p c e n", p=P)

            def expert_cols(w, pair, i):
                return w[:, bass.ds(pair * (2 * DC), 2 * DC), bass.ds(i * P, P)]

            def expert_rows(pair, i):
                return wd[:, bass.ds(i, 1), bass.ds(pair * 2, 2), :].squeeze(1)

            b0 = STREAM["moe"]
            load(b0, expert_cols(wg, 0, 0))
            load(b0 + 1, expert_cols(wu, 0, 0))
            with sp.Fori(1, FB) as i:
                load(b0 - 1, expert_cols(wg, 0, i), i)
                load(b0, expert_cols(wu, 0, i), i)
                load(b0 + 1, expert_rows(0, i - 1), i)
            with sp.Fori(1, E // 2) as pair:
                load(b0 - 1, expert_cols(wg, pair, 0), pair * FB)
                load(b0, expert_cols(wu, pair, 0), pair * FB)
                load(b0 + 1, expert_rows(pair - 1, FB - 1), pair * FB)
                with sp.Fori(1, FB) as i:
                    load(b0 - 1, expert_cols(wg, pair, i), pair * FB + i)
                    load(b0, expert_cols(wu, pair, i), pair * FB + i)
                    load(b0 + 1, expert_rows(pair, i - 1), pair * FB + i)
            b0 += 3 * FB * (E // 2)
            load(b0 - 1, expert_rows(E // 2 - 1, FB - 1))
            for j in range(2):
                load(b0 + j, a["o_router_w_2"][0].rearrange("(k p) n -> p k n", p=P)[:, :, 0:2])
            for t in range(TT):
                sp.wait_ge(out_copied, 2 * (t + 1))
                sp.dma_start(out[0, t * P:(t + 1) * P, :], XIN[:, t, :]).then_inc(out_stored, 16)
            sp.wait_ge(out_stored, 16 * TT)

        @block.gpsimd
        def _(pool):
            def ada(n):
                w = a["e_ada_w_2" if n < 2 else "o_ada_w_2"][0].rearrange("(k p) n -> p k n", p=P)
                dst = RAWA[:, :].rearrange("p (k n) -> p k n", k=DC)
                at = (n % 2) * 12 * BW
                hold(pool, ada_used, 12 * n)
                pool.dma_start(dst, w[:, :, at:at + BW]).then_inc(ada_landed, 16)
                with pool.Fori(1, 12) as i:
                    pool.wait_ge(ada_used, i + 12 * n)
                    pool.dma_start(dst, w[:, :, bass.ds(i * BW + at, BW)]).then_inc(ada_landed, 16)

            nc.gpsimd.memset(KRZ[:, :, :], 0.0).then_inc(zeroed, 1)
            for s in (at_score, at_max, at_exp, at_prob, at_turned, at_pt, at_pv, at_oh, at_ol):
                pool.sem_inc(s, GH)
            pool.sem_inc(at_q, 2)
            forget = a["e_w_in_2"][0].rearrange("(k p) n -> p k n", p=P)[:, :, 1536:1536 + FOXH]
            for dst, src in ((FG[:, :, :], forget), (RW[:, :, :], a["o_router_w_2"][0].rearrange("(k p) n -> p k n", p=P)),
                             (FB4[:, 0:1], a["e_forget_b_2"][0, 0:4].rearrange("(r n) -> r n", n=1)),
                             (FB4[:, 1:2], a["e_forget_b_2"][0, 4:8].rearrange("(r n) -> r n", n=1)),
                             (SINK[:, 0, :], a["e_sinks_2"].broadcast_to([P, FOXH])),
                             (RB[:, :], a["o_router_b_2"].broadcast_to([P, E])),
                             (POSI[:, :], a["positions_2"].broadcast_to([P, S]))):
                pool.dma_start(dst, src).then_inc(in_small, 16)
            for n in range(3):
                ada(n)
            pool.wait_ge(v_out, 8)
            pool.wait_ge(ada_used, 36)
            with pool.Fori(G_MLA, G_MLA + HEADS_A // GH) as g:
                pool.wait_ge(at_pv, g * GH)
                nc.gpsimd.tensor_copy(VS[:, :, :], V[:, :, bass.ds(g * (GH * VD) - GH * VD * G_MLA, GH * VD)]).then_inc(v_staged, 1)
            pool.wait_ge(at_pv, GH * G_FOX)
            ada(3)
            def pad_keys(index):
                for j in range(2):
                    other = slice(HD - HD * j, P - HD * j)
                    nc.gpsimd.memset(KZ[other, :, :].rearrange("p (h j) t -> p h j t", j=2)[:, :, j, :], 0.0)
                    ins = nc.gpsimd.memset(IKZ[other, j, :], 0.0) if index else None
                return ins

            pad_keys(True).then_inc(pads, 1)
            with pool.Fori(G_DSA, G_DSA + 4) as g:
                pool.wait_ge(at_pv, g * GH)
                pool.wait_ge(key_vec, 17)
                nc.gpsimd.tensor_copy(VSD[:, :, :], V2[:, :, bass.ds(g * P - P * G_DSA, P)]).then_inc(v_staged, 1)

        @block.scalar
        def _(act):
            chain = Chain(act, act_chain)

            def prep(c, i=0, moves=whole()):
                act.wait_ge(raw_landed[c % RING], i * 16 + 16 * (c // RING + 1))
                if not isinstance(i, int) or c >= RING:
                    act.wait_ge(w_used, i * 3 + (c - RING + 1))
                for src, dst in moves:
                    ins = nc.scalar.copy(dst(WH[c % RING]), src(RAW[c % RING]))
                ins.then_inc(hi_ready, 1)

            def norm_scaled(k, gain, free, stats=True):
                hold(act, w_used, free)
                for cp in range(4):
                    act.wait_ge(x_ready, 4 * k + cp + 1)
                    for c in (2 * cp, 2 * cp + 1):
                        nc.scalar.activation(UH[:, c, :], X[:, c, :], ACT.Identity,
                                             scale=gain[:, c:c + 1]).then_inc(u_hi, 1)
                    if stats:
                        nc.scalar.activation(T[:, 2 * cp:2 * cp + 2, :], X[:, 2 * cp:2 * cp + 2, :],
                                             ACT.Square).then_inc(sq_done, 1)

            def squares(k):
                for cp in range(4):
                    act.wait_ge(x_ready, 4 * k + cp + 1)
                    nc.scalar.activation(T[:, 2 * cp:2 * cp + 2, :], X[:, 2 * cp:2 * cp + 2, :],
                                         ACT.Square).then_inc(sq_done, 1)

            def root(s):
                act.wait_ge(var_inv, s + 1)
                nc.scalar.activation(R[:, :], RV[:, :], ACT.Sqrt).then_inc(r_done, 1)

            def ffn(n, name, s=None, scaled=True):
                b0, h0 = STREAM[name], FB * n

                def step(i, first=False):
                    g, u, d = (b0, b0 + 1, None) if first else (b0 - 1, b0, b0 + 1)
                    prep(g + 3, i)
                    if first and s is not None:
                        root(s)
                    if scaled:
                        act.wait_ge(g_free, i + (h0 + 1))
                    else:
                        act.wait_ge(w_used, i * 3 + (g + 1))
                    hold(act, h_done, i + h0)
                    nc.scalar.activation(SG[:, :], GS[:, :] if scaled else GB[:, :], ACT.Silu).then_inc(silu_done, 1)
                    prep(u + 3, i)
                    act.wait_ge(h_done, i + (h0 + 1))
                    nc.scalar.copy(HH[:, bass.ds((i % 2) * 2, 2), :], HF[:, :, :]).then_inc(h_hi, 1)
                    if d is not None:
                        prep(d + 3, i)

                step(0, True)
                with act.Fori(1, FB) as i:
                    step(i)
                prep(b0 + 3 * FB + 2)


            def group_probs(g, sink=None):
                for hh in range(GH):
                    act.wait_ge(at_max, g * GH + (hh + 1))
                    for t, (k0, k1) in enumerate(Q_TILES):
                        ins = nc.scalar.activation(PR[hh][:, k0:k1], PR[hh][:, k0:k1], ACT.Exp,
                                                   bias=SM[:, hh, t:t + 1], accum_out=SM[:, hh, 2 + t:3 + t])
                        if sink is not None:
                            ins = nc.scalar.activation(SM[:, hh, 4 + t:5 + t], SM[:, hh, t:t + 1], ACT.Exp,
                                                       bias=sink(g, hh))
                    ins.then_inc(at_exp, 1)

            def group_outputs(g, high):
                def turned_probs(hh):
                    act.wait_ge(at_turned, g * GH + (hh + 1))
                    act.wait_ge(at_pv, g * GH + (hh - 1))
                    nc.scalar.copy(PT[hh % 2][:, :], (GB, UB)[hh % 2][:, 0:P + S]).then_inc(at_pt, 1)

                def output(hh):
                    act.wait_ge(at_pv, g * GH + (hh + 1))
                    high(g, hh, (MB, SB)[hh % 2]).then_inc(at_oh, 1)

                turned_probs(0)
                turned_probs(1)
                output(0)
                turned_probs(2)
                output(1)
                turned_probs(3)
                output(2)
                output(3)

            for name, src in VEC_SRC.items():
                at, n = VEC[name]
                w = a[src].rearrange("l n -> (l n)") if len(a[src].shape) == 2 else a[src]
                act.dma_start(VR[at:at + n, :], w.rearrange("(r n) -> r n", n=P)).then_inc(in_vec, 16)
            for k, src in enumerate(("e_ada_b_2", "o_ada_b_2")):
                act.dma_start(AR[48 * k:48 * k + 48, :], a[src][0].rearrange("(r n) -> r n", n=P)).then_inc(in_vec, 16)
            act.dma_start(INVC[:, :, :], a["window_counts"].rearrange("p (g t) -> p g t", g=4)).then_inc(in_inv, 16)
            act.wait_ge(vec_ready, 2)
            nc.scalar.activation(CS[:, :], vec("c"), ACT.Silu).then_inc(c_ready, 1)
            for c in range(RING):
                prep(c)
            norm_scaled(0, vec("ffn_pre"), 0)
            ffn(0, "ffn0", 0)
            squares(1)
            root(1)
            for g in range(4):
                act.wait_ge(pooled, g + 1)
                nc.scalar.copy(UH[:, 2 * g:2 * g + 2, :], PY[:, :, :]).then_inc(u_hi, 2)
            prep(STREAM["pool"] + 3)
            norm_scaled(2, vec("ffn_post"), STREAM["pool"] + 1)
            ffn(1, "ffn1", 2)
            norm_scaled(3, vec("kv_in"), STREAM["dkv"])
            root(3)
            prep(STREAM["dkv"] + 3)
            act.wait_ge(kv_vec, 1)
            nc.scalar.activation(T[:, 0, :], T[:, 1, :], ACT.Square).then_inc(kv_act, 1)
            act.wait_ge(kv_vec, 9)
            nc.scalar.activation(T[:, 6, :], T[:, 5, :], ACT.Sqrt).then_inc(kv_act, 1)
            act.wait_ge(kv_vec, 10)
            nc.scalar.copy(CKH[:, :], T[:, 1, :]).then_inc(kv_act, 1)
            norm_scaled(3, vec("ffn_pre", DC), STREAM["dkv"] + 1, stats=False)
            ffn(2, "ffn2")
            norm_scaled(4, vec("mix", DC), STREAM["dq"])
            root(4)
            act.wait_ge(q_vec, 1)
            nc.scalar.activation(T[:, 2:4, :], T[:, 0:2, :], ACT.Square).then_inc(q_act, 1)
            act.wait_ge(q_vec, 3)
            nc.scalar.activation(T[:, 6, :], T[:, 5, :], ACT.Sqrt).then_inc(q_act, 1)
            for k in range(4):
                act.wait_ge(*((k_full, k + 1) if k < 3 else (w_used, STREAM["uk"] + 1)))
                nc.scalar.copy(KN[:, 4 * k:4 * k + 4, :],
                               ACC[:, (k % 2) * 1024:(k % 2) * 1024 + 1024].rearrange("p (h t) -> p h t", h=4)
                               ).then_inc(k_out, 1)
            act.wait_ge(q_vec, 5)
            act.wait_ge(w_used, STREAM["dq"] + 1)
            nc.scalar.copy(QCH, T[:, 0:2, :]).then_inc(q_act, 1)
            scale = float(NOPE + ROPE) ** -0.5
            with act.Fori(G_MLA, G_MLA + HEADS_A // GH) as g:
                for part, n in enumerate(UQ_PARTS):
                    prep(STREAM["uq"] + part, g - G_MLA, heads_apart(n // (NOPE + ROPE)))
                act.wait_ge(w_used, g * 3 + (STREAM["uq"] + 3 - 3 * G_MLA))
                nc.scalar.activation(T[:, 0:4, :], ACC[:, 0:1024].rearrange("p (h t) -> p h t", h=4),
                                     ACT.Copy, scale=scale).then_inc(at_q, 1)
                nc.scalar.activation(T[:, 6:8, :], ACC[:, 1024:1536].rearrange("p (h t) -> p h t", h=2),
                                     ACT.Copy, scale=scale).then_inc(at_q, 1)
                group_probs(g)
                group_outputs(g, lambda g, hh, bank: nc.scalar.copy(
                    OH[:, bass.ds(g * GH + (hh - GH * G_MLA), 1), :], bank[:, 0:S].unsqueeze(1)))
            b = STREAM["wo"]
            for k in range(3):
                prep(b + k)
            prep(b + 3)
            with act.Fori(0, 2) as i:
                for j in range(3):
                    prep(b + 4 + j, i)
            prep(b + 10)
            norm_scaled(5, vec("ffn_post", DC), b + 8)
            ffn(3, "ffn3", 5)
            def norm_modulated(n, shift, free):
                act.wait_ge(w_used, free)
                for c in range(DC):
                    act.wait_ge(normed, DC * (n - 7) + c + 1)
                    nc.scalar.activation(UH[:, c, :], T[:, c, :], ACT.Identity, bias=shift[:, c:c + 1],
                                         scale=ADA[:, c:c + 1]).then_inc(u_hi, 1)

            squares(6)
            root(6)
            act.wait_ge(trig_vec, 2)
            nc.scalar.activation(SINP[:, :], ANG[0][:, :], ACT.Sin)
            nc.scalar.activation(COSP[:, :], ANG[1][:, :], ACT.Sin).then_inc(trig_act, 1)
            squares(7)
            root(7)
            norm_modulated(7, MOD[:, 0:8], STREAM["ffn3"] + 3 * FB)
            prep(STREAM["fv"] + 1)
            act.wait_ge(fg_vec, 2)
            nc.scalar.activation(LM[:, :, :], LM[:, :, :], ACT.Exp, scale=-1.0).then_inc(fg_act, 1)
            act.wait_ge(fg_act, 1)
            nc.scalar.activation(LM[:, :, :], LM[:, :, :], ACT.Ln, bias=const("ones")[0:4, 0:1]).then_inc(fg_act, 1)
            for p in range(4):
                act.wait_ge(w_used, STREAM["fk"] + 1 + p // 2)
                act.wait_ge(pads, 1)
                for j in range(2):
                    half = slice(HD * j, HD * j + HD)
                    ins = nc.scalar.copy(KZ[half, 2 * p + j, :], (GB, UB)[p // 2][half, (p % 2) * S:(p % 2) * S + S])
            ins.then_inc(fg_act, 1)

            def queries(name, g, i, to, inc):
                for part, (k0, k1) in enumerate(Q_PARTS):
                    prep(STREAM[name] + part, i, whole((k1 - k0) * BW))
                act.wait_ge(w_used, i * 3 + (STREAM[name] + 3))
                nc.scalar.activation(to, ACC[:, 0:512].rearrange("p (h t) -> p h t", h=2),
                                     ACT.Copy, scale=float(HD) ** -0.5).then_inc(at_q, inc)

            def half_high(chunk):
                def high(g, hh, bank):
                    half = slice(HD * (hh % 2), HD * (hh % 2) + HD)
                    at = chunk(g, hh)
                    return nc.scalar.copy(OH[half, bass.ds(at, 1), :], bank[half, 0:S].unsqueeze(1))
                return high

            for g in range(G_FOX, G_FOX + 2):
                queries("fq", g, g - G_FOX, T[:, 4:6, :], 2)
                group_probs(g)
                group_outputs(g, half_high(lambda g, hh: (g - G_FOX) * 2 + hh // 2))
            prep(STREAM["skv"])
            for g in range(G_WIN, G_WIN + 2):
                queries("sq", g, g - G_WIN, T[:, 6:8, :], 2)
                group_probs(g, sink=lambda g, hh: SINK[:, 0, (g - G_WIN) * GH + hh:(g - G_WIN) * GH + hh + 1])
                group_outputs(g, half_high(lambda g, hh: 4 + (g - G_WIN) * 2 + hh // 2))
            b = STREAM["ewo"]
            for k in range(7):
                prep(b + k)
            squares(8)
            root(8)
            norm_modulated(8, MOD[:, 24:32], b + 4)
            ffn(4, "ffn4", scaled=False)
            squares(9)
            root(9)
            norm_modulated(9, MOD[:, 48:56], STREAM["ffn4"] + 3 * FB)
            prep(STREAM["dk"])
            prep(STREAM["dv"])
            for h in range(IH):
                act.wait_ge(ix_mm, h + 1)
                hold(act, ix_vec, h - 1)
                nc.scalar.activation(RL[h % 2][:, :], ACC[:, 512 * (h % 4):512 * (h % 4) + P + S],
                                     ACT.Relu).then_inc(ix_act, 1)
            with act.Fori(G_DSA, G_DSA + 4) as g:
                queries("dsq", g, g - G_DSA, T[:, 6:8, :], 2)
                group_probs(g)
                group_outputs(g, half_high(lambda g, hh: g * 2 + (hh // 2 - 2 * G_DSA)))
            b = STREAM["owo"]
            for k in range(7):
                prep(b + k)
            squares(10)
            root(10)
            norm_modulated(10, MOD[:, 72:80], b + 4)
            act.wait_ge(rt_vec, 5)
            nc.scalar.activation(GATE[:, :, 1:2], GATE[:, :, 0:1], ACT.Exp).then_inc(rt_act, 1)

            def experts(n, first=False):
                g, u, d = (STREAM["moe"], STREAM["moe"] + 1, None) if first else (
                    STREAM["moe"] - 1, STREAM["moe"], STREAM["moe"] + 1)
                h0 = 5 * FB
                prep(g + 3, n)
                act.wait_ge(w_used, n * 3 + (g + 1))
                act.wait_ge(h_done, n + h0)
                nc.scalar.activation(SG[:, :], GB[:, :], ACT.Silu).then_inc(silu_done, 1)
                prep(u + 3, n)
                act.wait_ge(h_done, n + (h0 + 1))
                nc.scalar.copy(HH[:, bass.ds(((n + 1) % 2) * 2, 2), :], HF[:, :, :]).then_inc(h_hi, 1)
                if d is not None:
                    prep(d + 3, n)

            experts(0, True)
            with act.Fori(1, FB * (E // 2)) as n:
                experts(n)
            squares(11)
            root(11)

        @block.vector
        def _(dve):
            chain = Chain(dve, dve_chain)

            def prep(c, i=0, moves=whole()):
                dve.wait_ge(hi_ready, i * 3 + (c + 1))
                for src, dst in moves:
                    ins = nc.vector.tensor_tensor(dst(WL[c % RING]), src(RAW[c % RING]),
                                                  dst(WH[c % RING]).bitcast(F32), ALU.subtract)
                ins.then_inc(lo_ready, 1)

            def used(c, i=0):
                dve.wait_ge(w_used, i * 3 + (c + 1))

            def low_scaled(n, gain):
                for c in range(DC):
                    dve.wait_ge(u_hi, DC * n + c + 1)
                    nc.vector.scalar_tensor_tensor(UL[:, c, :], X[:, c, :], gain[:, c:c + 1],
                                                   UH[:, c, :].bitcast(F32), ALU.mult, ALU.subtract).then_inc(u_lo, 1)

            def sums(s):
                dve.wait_ge(sq_done, 4 * s + 4)
                chain.link(nc.vector.tensor_tensor(SS[:, :].rearrange("p (k t) -> p k t", k=2), T[:, 0:2, :],
                                                   T[:, 2:4, :], ALU.add))
                chain.link(nc.vector.tensor_tensor(SS[:, :].rearrange("p (k t) -> p k t", k=2),
                                                   SS[:, :].rearrange("p (k t) -> p k t", k=2),
                                                   T[:, 4:6, :], ALU.add))
                nc.vector.tensor_tensor(SS[:, :].rearrange("p (k t) -> p k t", k=2),
                                        SS[:, :].rearrange("p (k t) -> p k t", k=2),
                                        T[:, 6:8, :], ALU.add).then_inc(ss_done, 1)

            def inverse(s):
                dve.wait_ge(stats_done, s + 1)
                chain.link(nc.vector.tensor_scalar(RV[:, :], SB[:, 0:S], 1.0 / D, EPS, ALU.mult, ALU.add))
                nc.vector.reciprocal(RV[:, :], RV[:, :]).then_inc(var_inv, 1)

            def add_product(c, i=0, factor=None, gain=None):
                for cp in range(4):
                    if cp < 3:
                        dve.wait_ge(acc_full, 3 * add_product.n + cp + 1)
                    else:
                        used(c, i)
                    acc = ACC[:, 512 * cp:512 * cp + 512].rearrange("p (k t) -> p k t", k=2)
                    x = X[:, 2 * cp:2 * cp + 2, :]
                    if gain is None:
                        nc.vector.scalar_tensor_tensor(x, acc, factor, x, ALU.mult, ALU.add).then_inc(x_ready, 1)
                    else:
                        for j in range(2):
                            k = 2 * cp + j
                            ins = nc.vector.scalar_tensor_tensor(X[:, k, :], acc[:, j, :], gain[:, k:k + 1],
                                                                 X[:, k, :], ALU.mult, ALU.add)
                        ins.then_inc(x_ready, 1)
                add_product.n += 1

            add_product.n = 0

            def two(ap):
                return ap.rearrange("p (k t) -> p k t", k=2)

            def ffn(n, name, s=None, scaled=True, ada=True):
                b0, h0 = STREAM[name], FB * n

                def step(i, first=False):
                    g, u, d = (b0, b0 + 1, None) if first else (b0 - 1, b0, b0 + 1)
                    if first and s is not None:
                        inverse(s)
                        dve.wait_ge(r_done, s + 1)
                    used(g, i)
                    if scaled:
                        hold(dve, silu_done, i + h0)
                        nc.vector.tensor_tensor(two(GS[:, :]), two(GB[:, :]), wide(R[:, :], 2),
                                                ALU.mult).then_inc(g_free, 1)
                    prep(g + 3, i)
                    used(u, i)
                    if scaled:
                        hold(dve, h_done, i + h0)
                        nc.vector.tensor_tensor(two(US[:, :]), two(UB[:, :]), wide(R[:, :], 2),
                                                ALU.mult).then_inc(u_free, 1)
                        dve.wait_ge(u_free, i + (h0 + 1))
                    dve.wait_ge(silu_done, i + (h0 + 1))
                    hold(dve, h_lo, i + h0)
                    nc.vector.tensor_tensor(HF[:, :, :], two(SG[:, :]), two(US[:, :] if scaled else UB[:, :]),
                                            ALU.mult).then_inc(h_done, 1)
                    prep(u + 3, i)
                    dve.wait_ge(h_hi, i + (h0 + 1))
                    nc.vector.tensor_tensor(HL[:, bass.ds((i % 2) * 2, 2), :], HF[:, :, :],
                                            HH[:, bass.ds((i % 2) * 2, 2), :].bitcast(F32),
                                            ALU.subtract).then_inc(h_lo, 1)
                    if d is not None:
                        prep(d + 3, i)
                    if ada:
                        modulation(i)

                def modulation(i):
                    dve.wait_ge(ada_used, i + (12 * n + 1))
                    at = bass.ds(i * 2 + 24 * n, 2)
                    nc.vector.tensor_tensor(MOD[:, at], MB[:, 0:2], ABT[:, at], ALU.add).then_inc(ada_read, 1)

                step(0, True)
                with dve.Fori(1, FB) as i:
                    step(i)
                if ada:
                    modulation(FB)

            def rope(g, raw, to, cos, sin, off):
                chain.link(nc.vector.tensor_tensor(to, raw, wide(cos, 2), ALU.mult))
                dve.wait_ge(at_rot, g + off)
                chain.link(nc.vector.tensor_tensor(raw, two(MB[:, :]), wide(sin, 2), ALU.mult))
                nc.vector.tensor_tensor(to, to, raw, ALU.add).then_inc(at_qr, 1)

            def group_scores(g, mask, row_bias=None, sink=None):
                for hh in range(GH):
                    dve.wait_ge(at_score, g * GH + (hh + 1))
                    bank = ACC[:, 512 * hh:512 * hh + P + S]
                    if row_bias is None:
                        chain.link(nc.vector.tensor_tensor(PR[hh][:, :], bank, mask, ALU.add))
                    else:
                        for t, (k0, k1) in enumerate(Q_TILES):
                            chain.link(nc.vector.scalar_tensor_tensor(
                                PR[hh][:, k0:k1], bank[:, k0:k1], row_bias(g, hh, t), mask[:, k0:k1], ALU.add, ALU.add))
                    for t, (k0, k1) in enumerate(Q_TILES):
                        ins = nc.vector.tensor_reduce(SM[:, hh, t:t + 1], PR[hh][:, k0:k1], AX_X, ALU.max, negate=True)
                    if sink is not None:
                        chain.link(ins)
                        ins = nc.vector.tensor_scalar(SM[:, hh, 0:2], SM[:, hh, 0:2], sink(g, hh), None, ALU.min)
                    ins.then_inc(at_max, 1)

            def group_outputs(g, low, sink=False):
                def probs(hh):
                    dve.wait_ge(at_exp, g * GH + (hh + 1))
                    if sink:
                        chain.link(nc.vector.tensor_tensor(SM[:, hh, 2:4], SM[:, hh, 2:4], SM[:, hh, 4:6], ALU.add))
                    chain.link(nc.vector.reciprocal(SM[:, hh, 6:8], SM[:, hh, 2:4]))
                    for t, (k0, k1) in enumerate(Q_TILES):
                        ins = nc.vector.tensor_scalar(PR[hh][:, k0:k1], PR[hh][:, k0:k1], SM[:, hh, 6 + t:7 + t],
                                                      None, ALU.mult)
                    ins.then_inc(at_prob, 1)

                def output(hh):
                    dve.wait_ge(at_oh, g * GH + (hh + 1))
                    low(g, hh, (MB, SB)[hh % 2]).then_inc(at_ol, 1)

                probs(0)
                probs(1)
                probs(2)
                output(0)
                probs(3)
                output(1)
                output(2)
                output(3)

            for cp in range(4):
                dve.wait_ge(turned, cp + 1)
                nc.vector.tensor_copy(X[:, 2 * cp:2 * cp + 2, :], two(ACC[:, 512 * cp:512 * cp + 512])).then_inc(x_ready, 1)
            dve.wait_ge(turned, 5)
            nc.vector.tensor_copy(VT[:, :], MB[:, 0:NV]).then_inc(vec_ready, 1)
            dve.wait_ge(turned, 6)
            nc.vector.tensor_copy(ABT[:, :], SB[:, 0:NA]).then_inc(vec_ready, 1)
            dve.wait_ge(vec_ready, 2)
            for c in range(RING):
                prep(c)
            low_scaled(0, vec("ffn_pre"))
            sums(0)
            ffn(0, "ffn0", 0)
            add_product(STREAM["ffn0"] + 3 * FB - 1, factor=0.5)
            prep(STREAM["ffn0"] + 3 * FB + 2)
            sums(1)
            inverse(1)
            dve.wait_ge(r_done, 2)
            for k in range(2):
                chain.link(nc.vector.memset(PB[k][:, :, 0:8], 0.0))
            for c in range(DC):
                chain.link(nc.vector.scalar_tensor_tensor(T[:, c, :], X[:, c, :], vec("mix")[:, c:c + 1], R[:, :],
                                                          ALU.mult, ALU.mult))
            dve.wait_ge(in_inv, 16)
            for g in range(4):
                u = T[:, 2 * g:2 * g + 2, :]
                chain.link(nc.vector.tensor_copy(PB[0][:, :, 8:], u))
                k, lag = 0, 1
                while lag < 2 ** (g + 1):
                    chain.link(nc.vector.tensor_tensor(PB[1 - k][:, :, 8:], PB[k][:, :, 8:],
                                                       PB[k][:, :, 8 - lag:8 + S - lag], ALU.add))
                    k, lag = 1 - k, 2 * lag
                dve.wait_ge(u_lo, DC + 2 * g)
                chain.link(nc.vector.tensor_tensor(PY[:, :, :], PB[k][:, :, 8:], wide(INVC[:, g, :], 2), ALU.mult))
                nc.vector.tensor_tensor(PY[:, :, :], PY[:, :, :], u, ALU.subtract).then_inc(pooled, 1)
                dve.wait_ge(u_hi, DC + 2 * g + 2)
                nc.vector.tensor_tensor(UL[:, 2 * g:2 * g + 2, :], PY[:, :, :],
                                        UH[:, 2 * g:2 * g + 2, :].bitcast(F32), ALU.subtract).then_inc(u_lo, 2)
            add_product(STREAM["pool"], gain=vec("pool_scale"))
            prep(STREAM["pool"] + 3)
            low_scaled(2, vec("ffn_post"))
            sums(2)
            ffn(1, "ffn1", 2)
            add_product(STREAM["ffn1"] + 3 * FB - 1, factor=0.5)
            prep(STREAM["ffn1"] + 3 * FB + 2)
            low_scaled(3, vec("kv_in"))
            sums(3)
            inverse(3)
            used(STREAM["dkv"])
            dve.wait_ge(r_done, 4)
            nc.vector.tensor_tensor(T[:, 1, :], GB[:, 0:S], R[:, :], ALU.mult).then_inc(kv_vec, 1)
            nc.vector.tensor_tensor(T[0:ROPE, 7, :], UB[0:ROPE, 0:S], R[0:ROPE, :], ALU.mult).then_inc(kv_vec, 1)
            dve.wait_ge(kv_mm, 1)
            nc.vector.tensor_copy(T[:, 2, :], GB[:, S:]).then_inc(kv_vec, 1)
            dve.wait_ge(kv_mm, 2)
            nc.vector.tensor_tensor(T[:, 4, :], MB[:, 0:S], const("sin"), ALU.mult).then_inc(kv_vec, 1)
            nc.vector.tensor_tensor(T[:, 2, :], T[:, 2, :], const("cos"), ALU.mult).then_inc(kv_vec, 1)
            dve.wait_ge(kv_vec, 5)
            dve.wait_ge(zeroed, 1)
            for k in range(2):
                half = slice(64 * k, 64 * k + 64)
                nc.vector.tensor_tensor(KRZ[half, k, :], T[half, 2, :], T[half, 4, :], ALU.add).then_inc(kv_vec, 1)
            dve.wait_ge(kv_mm, 3)
            nc.vector.tensor_scalar(T[:, 3, :], SB[:, 0:S], 1.0 / KVL, EPS, ALU.mult, ALU.add).then_inc(kv_vec, 1)
            dve.wait_ge(kv_vec, 8)
            nc.vector.reciprocal(T[:, 5, :], T[:, 3, :]).then_inc(kv_vec, 1)
            dve.wait_ge(kv_act, 2)
            nc.vector.scalar_tensor_tensor(T[:, 1, :], T[:, 1, :], vec("ckv", 0, 1), T[:, 6, :],
                                           ALU.mult, ALU.mult).then_inc(kv_vec, 1)
            dve.wait_ge(kv_act, 3)
            nc.vector.tensor_tensor(CKL[:, :], T[:, 1, :], CKH[:, :].bitcast(F32), ALU.subtract).then_inc(kv_vec, 1)
            prep(STREAM["dkv"] + 3)
            low_scaled(4, vec("ffn_pre", DC))
            ffn(2, "ffn2")
            add_product(STREAM["ffn2"] + 3 * FB - 1, factor=0.5)
            prep(STREAM["ffn2"] + 3 * FB + 2)
            low_scaled(5, vec("mix", DC))
            sums(4)
            inverse(4)
            used(STREAM["dq"])
            dve.wait_ge(r_done, 5)
            nc.vector.tensor_tensor(T[:, 0:2, :], two(GB[:, :]), wide(R[:, :], 2), ALU.mult).then_inc(q_vec, 1)
            dve.wait_ge(q_mm, 1)
            nc.vector.tensor_scalar(T[:, 4, :], SB[:, 0:S], 1.0 / QL, EPS, ALU.mult, ALU.add).then_inc(q_vec, 1)
            dve.wait_ge(q_vec, 2)
            nc.vector.reciprocal(T[:, 5, :], T[:, 4, :]).then_inc(q_vec, 1)
            dve.wait_ge(q_act, 2)
            for k in range(2):
                nc.vector.scalar_tensor_tensor(T[:, k, :], T[:, k, :], vec("q_lora", k, 1), T[:, 6, :],
                                               ALU.mult, ALU.mult).then_inc(q_vec, 1)
            dve.wait_ge(q_act, 3)
            nc.vector.tensor_tensor(QCL, T[:, 0:2, :], QCH.bitcast(F32), ALU.subtract).then_inc(q_vec, 1)
            for j in range(8):
                dve.wait_ge(*((v_full, j + 1) if j < 7 else (w_used, STREAM["uv"] + 1)))
                nc.vector.tensor_copy(V[:, j // 4, 512 * (j % 4):512 * (j % 4) + 512],
                                      (GB, UB)[j % 2][:, :]).then_inc(v_out, 1)
            with dve.Fori(G_MLA, G_MLA + HEADS_A // GH) as g, chain.laps(g - G_MLA, 4, 10):
                for part, n in enumerate(UQ_PARTS):
                    prep(STREAM["uq"] + part, g - G_MLA, heads_apart(n // (NOPE + ROPE)))
                dve.wait_ge(at_q, g * 2 + 2)
                rope(g, T[:, 6:8, :], T[:, 4:6, :], const("cos"), const("sin"), 1 - G_MLA)
                group_scores(g, const("causal"))
                group_outputs(g, lambda g, hh, bank: nc.vector.tensor_tensor(
                    OL[:, bass.ds(g * GH + (hh - GH * G_MLA), 1), :], bank[:, 0:S].unsqueeze(1),
                    OH[:, bass.ds(g * GH + (hh - GH * G_MLA), 1), :].bitcast(F32), ALU.subtract))
            b = STREAM["wo"]
            for k in range(3):
                prep(b + k)
            prep(b + 3)
            with dve.Fori(0, 2) as i:
                for j in range(3):
                    prep(b + 4 + j, i)
            add_product(b + 7, factor=1.0)
            prep(b + 10)
            low_scaled(6, vec("ffn_post", DC))
            sums(5)
            ffn(3, "ffn3", 5)
            add_product(STREAM["ffn3"] + 3 * FB - 1, factor=0.5)
            def norm_in_place(s, k, gain):
                sums(s)
                inverse(s)
                dve.wait_ge(r_done, s + 1)
                for c in range(DC):
                    ins = nc.vector.scalar_tensor_tensor(X[:, c, :], X[:, c, :], gain[:, c:c + 1], R[:, :],
                                                         ALU.mult, ALU.mult)
                    if c % 2:
                        ins.then_inc(x_ready, 1)

            def norm_modulated(n, gain, scale, shift):
                sums(n)
                inverse(n)
                if n == 7:
                    dve.wait_ge(ada_read, 48)
                dve.wait_ge(u_hi, DC * n)
                chain.link(nc.vector.scalar_tensor_tensor(ADA[:, :], scale, 1.0, gain, ALU.add, ALU.mult))
                dve.wait_ge(r_done, n + 1)
                for c in range(DC):
                    nc.vector.tensor_tensor(T[:, c, :], X[:, c, :], R[:, :], ALU.mult).then_inc(normed, 1)
                for c in range(DC):
                    dve.wait_ge(u_hi, DC * n + c + 1)
                    chain.link(nc.vector.tensor_scalar(T[:, c, :], T[:, c, :], ADA[:, c:c + 1], shift[:, c:c + 1],
                                                       ALU.mult, ALU.add))
                    nc.vector.tensor_tensor(UL[:, c, :], T[:, c, :], UH[:, c, :].bitcast(F32),
                                            ALU.subtract).then_inc(u_lo, 1)

            prep(STREAM["ffn3"] + 3 * FB + 2)
            norm_in_place(6, 6, vec("final1"))
            dve.wait_ge(in_small, 16 * N_SMALL)
            chain.link(nc.vector.tensor_copy(COSP[:, :], POSI[:, :]))
            chain.link(nc.vector.tensor_scalar(ANG[0][:, :], COSP[:, :], const("inv_freq"), None, ALU.mult))
            chain.link(nc.vector.tensor_scalar(SINP[:, :], ANG[0][:, :], 1.0 / (2.0 * np.pi), ROUND, ALU.mult, ALU.add))
            chain.link(nc.vector.tensor_scalar(SINP[:, :], SINP[:, :], -ROUND, None, ALU.add))
            for part in TURN:
                chain.link(nc.vector.scalar_tensor_tensor(ANG[0][:, :], SINP[:, :], -part, ANG[0][:, :],
                                                          ALU.mult, ALU.add))
            chain.link(nc.vector.tensor_scalar(ANG[0][:, :], ANG[0][:, :], HALF_TURN, -HALF_TURN, ALU.min, ALU.max))
            nc.vector.tensor_scalar(SINK[:, 1, :], SINK[:, 0, :], -1.0, None, ALU.mult).then_inc(trig_vec, 1)
            chain.link(nc.vector.scalar_tensor_tensor(ANG[1][:, :], ANG[0][:, :], -1.0, ANG[0][:, :], ALU.mult, ALU.max))
            nc.vector.tensor_scalar(ANG[1][:, :], ANG[1][:, :], -1.0, float(np.pi / 2), ALU.mult, ALU.add).then_inc(trig_vec, 1)
            norm_modulated(7, vec("e_mix"), MOD[:, 8:16], MOD[:, 0:8])
            prep(STREAM["fv"] + 1)
            dve.wait_ge(fg_mm, 1)
            for g in range(2):
                ins = nc.vector.tensor_scalar(LX[:, g, :], MB[0:4, g * S:(g + 1) * S], FB4[:, g:g + 1], None, ALU.add)
            ins.then_inc(fg_vec, 1)
            dve.wait_ge(fg_vec, 1)
            nc.vector.scalar_tensor_tensor(LM[:, :, :], LX[:, :, :], -1.0, LX[:, :, :], ALU.mult, ALU.max).then_inc(fg_vec, 1)
            dve.wait_ge(fg_act, 2)
            chain.link(nc.vector.scalar_tensor_tensor(LX[:, :, :], LX[:, :, :], 0.0, LM[:, :, :], ALU.min, ALU.subtract))
            for g in range(2):
                ins = nc.vector.tensor_tensor_scan(CUM[:, g, :], const("ones")[0:4, 0:1].broadcast_to([4, S]), LX[:, g, :],
                                                 0.0, ALU.mult, ALU.add)
            ins.then_inc(fg_vec, 1)
            used(STREAM["fv"] + 1)
            for t in range(TT):
                nc.vector.tensor_copy(V2[:, t, :], ACC[:, 512 * t:512 * t + 512])
            dve.wait_ge(fg_mm, 2)
            nc.vector.tensor_copy(CIT[:, :, :, :].rearrange("p g t h -> p (g t h)"), SB[:, 0:4 * GH]).then_inc(fg_vec, 1)
            dve.wait_ge(fg_vec, 4)

            def query_parts(name, i):
                for part, (k0, k1) in enumerate(Q_PARTS):
                    prep(STREAM[name] + part, i, whole((k1 - k0) * BW))

            def half_low(chunk):
                def low(g, hh, bank):
                    half = slice(HD * (hh % 2), HD * (hh % 2) + HD)
                    at = chunk(g, hh)
                    return nc.vector.tensor_tensor(OL[half, bass.ds(at, 1), :], bank[half, 0:S].unsqueeze(1),
                                                   OH[half, bass.ds(at, 1), :].bitcast(F32), ALU.subtract)
                return low

            for g in range(G_FOX, G_FOX + 2):
                query_parts("fq", g - G_FOX)
                group_scores(g, const("causal"),
                             row_bias=lambda g, hh, t: CIT[:, g - G_FOX, t, hh:hh + 1])
                group_outputs(g, half_low(lambda g, hh: (g - G_FOX) * 2 + hh // 2))
            prep(STREAM["skv"])
            used(STREAM["skv"])
            nc.vector.tensor_copy(T[:, 0, :], GB[:, 0:S]).then_inc(key_vec, 1)
            for t in range(TT):
                for j in range(2):
                    nc.vector.tensor_copy(V2[:, t, 0:2 * P].rearrange("p (h j n) -> p h j n", h=2, j=2)[:, :, j, :],
                                          GB[:, S + t * P:S + (t + 1) * P].rearrange("p (h n) -> p h n", h=2)
                                          ).then_inc(key_vec, 1)
            dve.wait_ge(trig_act, 1)
            dve.wait_ge(key_vec, 1)
            nc.vector.tensor_tensor(T[:, 1, :], T[:, 0, :], COSP[:, :], ALU.mult)
            dve.wait_ge(key_mm, 1)
            nc.vector.tensor_tensor(T[:, 2, :], MB[:, 0:S], SINP[:, :], ALU.mult).then_inc(key_vec, 1)
            dve.wait_ge(key_vec, 6)
            nc.vector.tensor_tensor(T[:, 1, :], T[:, 1, :], T[:, 2, :], ALU.add).then_inc(key_vec, 1)
            dve.wait_ge(key_vec, 7)
            low_half, high_half = slice(0, HD), slice(HD, P)
            nc.vector.tensor_copy(KZ[low_half, 0, :], T[low_half, 1, :])
            nc.vector.tensor_copy(KZ[high_half, 3, :], T[high_half, 1, :])
            dve.wait_ge(key_mm, 2)
            nc.vector.tensor_copy(KZ[low_half, 2, :], UB[low_half, 0:S])
            nc.vector.tensor_copy(KZ[high_half, 1, :], UB[high_half, 0:S]).then_inc(key_vec, 1)
            for g in range(G_WIN, G_WIN + 2):
                query_parts("sq", g - G_WIN)
                dve.wait_ge(at_q, g * 2 + 2)
                rope(g, T[:, 6:8, :], T[:, 4:6, :], COSP[:, :], SINP[:, :], -2)
                group_scores(g, const("window"),
                             sink=lambda g, hh: SINK[:, 1, (g - G_WIN) * GH + hh:(g - G_WIN) * GH + hh + 1])
                group_outputs(g, half_low(lambda g, hh: 4 + (g - G_WIN) * 2 + hh // 2), sink=True)
            b = STREAM["ewo"]
            for k in range(7):
                prep(b + k)
            add_product(b + 3, gain=MOD[:, 16:24])
            norm_modulated(8, vec("e_ffn"), MOD[:, 32:40], MOD[:, 24:32])
            ffn(4, "ffn4", scaled=False, ada=False)
            add_product(STREAM["ffn4"] + 3 * FB - 1, gain=MOD[:, 40:48])
            prep(STREAM["ffn4"] + 3 * FB + 2)
            norm_modulated(9, vec("o_mix"), MOD[:, 56:64], MOD[:, 48:56])
            prep(STREAM["dk"])
            prep(STREAM["dv"])
            used(STREAM["iq"] + 1)
            nc.vector.tensor_copy(T[:, 0:2, :], two(GB[:, :])).then_inc(key_vec, 1)
            nc.vector.tensor_copy(T[:, 2:4, :], two(UB[:, :])).then_inc(key_vec, 1)
            used(STREAM["ikw"])
            nc.vector.tensor_copy(T[0:HD, 6, :], ACC[0:HD, 0:S]).then_inc(key_vec, 1)
            used(STREAM["dk"])
            nc.vector.tensor_copy(T[:, 4:6, :], two(ACC[:, 1024:1536])).then_inc(key_vec, 1)
            nc.vector.tensor_scalar(IWT[:, :, :].rearrange("p t h -> p (t h)"), ACC[:, 512:512 + TT * IH],
                                    float(IH) ** -0.5 * float(HD) ** -0.5, None, ALU.mult).then_inc(key_vec, 1)
            used(STREAM["dv"])
            for t in range(TT):
                for j in range(2):
                    nc.vector.tensor_copy(V2[:, t, :].rearrange("p (h j n) -> p h j n", h=4, j=2)[:, :, j, :],
                                          ACC[:, 1536 + t * S:1536 + (t + 1) * S].rearrange("p (h n) -> p h n", h=4)
                                          ).then_inc(key_vec, 1)
            dve.wait_ge(key_vec, 17)
            for j, bank in enumerate((MB, SB)):
                chain.link(nc.vector.tensor_tensor(IQ[:, 2 * j:2 * j + 2, :], T[:, 2 * j:2 * j + 2, :],
                                                   wide(COSP[:, :], 2), ALU.mult))
                dve.wait_ge(key_mm, 3 + j)
                chain.link(nc.vector.tensor_tensor(T[:, 2 * j:2 * j + 2, :], two(bank[:, :]),
                                                   wide(SINP[:, :], 2), ALU.mult))
                nc.vector.tensor_tensor(IQ[:, 2 * j:2 * j + 2, :], IQ[:, 2 * j:2 * j + 2, :],
                                        T[:, 2 * j:2 * j + 2, :], ALU.add).then_inc(key_vec, 1)
            dve.wait_ge(key_mm, 5)
            nc.vector.tensor_copy(T[:, 6, :], GB[:, 0:S]).then_inc(key_vec, 1)
            dve.wait_ge(key_vec, 20)
            chain.link(nc.vector.tensor_tensor(T[:, 0:3, :], T[:, 4:7, :], wide(COSP[:, :], 3), ALU.mult))
            dve.wait_ge(key_mm, 6)
            nc.vector.tensor_tensor(T[:, 4:6, :], two(UB[:, :]), wide(SINP[:, :], 2), ALU.mult)
            chain.link(nc.vector.tensor_tensor(T[:, 6, :], GB[:, S:], SINP[:, :], ALU.mult))
            nc.vector.tensor_tensor(T[:, 0:3, :], T[:, 0:3, :], T[:, 4:7, :], ALU.add).then_inc(key_vec, 1)
            dve.wait_ge(key_vec, 21)
            dve.wait_ge(pads, 1)
            nc.vector.tensor_copy(IKZ[low_half, 0, :], T[low_half, 2, :])
            nc.vector.tensor_copy(IKZ[high_half, 1, :], T[high_half, 2, :]).then_inc(key_vec, 1)
            for p in range(2):
                nc.vector.tensor_copy(KZ[low_half, 4 * p, :], T[low_half, p, :])
                nc.vector.tensor_copy(KZ[high_half, 4 * p + 3, :], T[high_half, p, :])
            dve.wait_ge(key_mm, 7)
            for p in range(2):
                nc.vector.tensor_copy(KZ[low_half, 4 * p + 2, :], MB[low_half, p * S:(p + 1) * S])
                ins = nc.vector.tensor_copy(KZ[high_half, 4 * p + 1, :], MB[high_half, p * S:(p + 1) * S])
            ins.then_inc(key_vec, 1)
            for h in range(IH):
                dve.wait_ge(ix_act, h + 1)
                hold(dve, ix_vec, h)
                for t, (k0, k1) in enumerate(Q_TILES):
                    w = IWT[:, t, h:h + 1]
                    if h == 0:
                        ins = nc.vector.tensor_scalar(W[:, k0:k1], RL[0][:, k0:k1], w, None, ALU.mult)
                    else:
                        ins = nc.vector.scalar_tensor_tensor(W[:, k0:k1], RL[h % 2][:, k0:k1], w, W[:, k0:k1],
                                                             ALU.mult, ALU.add)
                ins.then_inc(ix_vec, 1)
            dve.wait_ge(ix_vec, IH)
            chain.link(nc.vector.tensor_tensor(W[:, :], W[:, :], const("causal"), ALU.add))
            for _ in range(TOPK // 8):
                for k0, k1 in Q_TILES:
                    chain.link(nc.vector.max(M8[:, :], W[:, k0:k1]))
                    chain.link(nc.vector.match_replace(W[:, k0:k1], M8[:, :], W[:, k0:k1], TAKEN))
            chain.link(nc.vector.tensor_scalar(SEL[:, :], W[:, :], TAKEN / 2, NEG, ALU.is_gt, ALU.mult))
            chain.link(nc.vector.tensor_tensor(SEL[:, :], SEL[:, :], const("causal"), ALU.add))
            with dve.Fori(G_DSA, G_DSA + 4) as g, chain.laps(g - G_DSA, 4, 10):
                query_parts("dsq", g - G_DSA)
                dve.wait_ge(at_q, g * 2 + 2)
                rope(g, T[:, 6:8, :], T[:, 4:6, :], COSP[:, :], SINP[:, :], -2)
                group_scores(g, SEL[:, :])
                group_outputs(g, half_low(lambda g, hh: g * 2 + (hh // 2 - 2 * G_DSA)))
            b = STREAM["owo"]
            for k in range(7):
                prep(b + k)
            add_product(b + 3, gain=MOD[:, 64:72])
            norm_modulated(10, vec("o_ffn"), MOD[:, 80:88], MOD[:, 72:80])
            dve.wait_ge(rt_mm, 1)
            nc.vector.tensor_tensor(LG[:, :, :], MB[:, 0:TT * E].rearrange("p (t e) -> p t e", t=TT),
                                    RB[:, :].unsqueeze(1).broadcast_to([P, TT, E]), ALU.add).then_inc(rt_vec, 1)
            dve.wait_ge(rt_vec, 1)
            for t in range(TT):
                ins = nc.vector.max(TOP[:, t, :], LG[:, t, :])
            ins.then_inc(rt_vec, 1)
            dve.wait_ge(rt_vec, 2)
            for t in range(TT):
                ins = nc.vector.max_index(TOPI[:, t, :], TOP[:, t, :], LG[:, t, :])
            ins.then_inc(rt_vec, 1)
            dve.wait_ge(rt_vec, 3)
            nc.vector.tensor_copy(TOPF[:, :, :], TOPI[:, :, :]).then_inc(rt_vec, 1)
            nc.vector.tensor_tensor(GATE[:, :, 0:1], TOP[:, :, 1:2], TOP[:, :, 0:1], ALU.subtract).then_inc(rt_vec, 1)
            dve.wait_ge(rt_act, 1)
            chain.link(nc.vector.tensor_scalar(GATE[:, :, 2:3], GATE[:, :, 1:2], 1.0, None, ALU.add))
            chain.link(nc.vector.reciprocal(GATE[:, :, 2:3], GATE[:, :, 2:3]))
            chain.link(nc.vector.tensor_tensor(GATE[:, :, 3:4], GATE[:, :, 1:2], GATE[:, :, 2:3], ALU.mult))
            for t in range(TT):
                for j, one in enumerate((ONE1, COMBT)):
                    ins = nc.vector.tensor_scalar(one[:, t, :], const("numbers"), TOPF[:, t, j:j + 1],
                                                  GATE[:, t, 2 + j:3 + j], ALU.is_equal, ALU.mult)
            chain.link(ins)
            nc.vector.tensor_tensor(COMBT[:, :, :], COMBT[:, :, :], ONE1[:, :, :], ALU.add).then_inc(rt_vec, 1)
            dve.wait_ge(rt_mm, 2)
            nc.vector.tensor_copy(T[:, :, :], ACC[:, :].rearrange("p (e t) -> p e t", e=E)).then_inc(rt_vec, 1)
            dve.wait_ge(rt_vec, 7)

            def experts(n, pair, first=False):
                g, u, d = (STREAM["moe"], STREAM["moe"] + 1, None) if first else (
                    STREAM["moe"] - 1, STREAM["moe"], STREAM["moe"] + 1)
                h0, u0 = 5 * FB, 4 * FB
                prep(g + 3, n)
                used(u, n)
                dve.wait_ge(h_done, n + h0)
                nc.vector.tensor_tensor(two(US[:, :]), two(UB[:, :]), T[:, bass.ds(pair * 2, 2), :],
                                        ALU.mult).then_inc(u_free, 1)
                dve.wait_ge(u_free, n + (u0 + 1))
                dve.wait_ge(silu_done, n + (h0 + 1))
                dve.wait_ge(h_lo, n + h0)
                nc.vector.tensor_tensor(HF[:, :, :], two(SG[:, :]), two(US[:, :]), ALU.mult).then_inc(h_done, 1)
                prep(u + 3, n)
                dve.wait_ge(h_hi, n + (h0 + 1))
                nc.vector.tensor_tensor(HL[:, bass.ds(((n + 1) % 2) * 2, 2), :], HF[:, :, :],
                                        HH[:, bass.ds(((n + 1) % 2) * 2, 2), :].bitcast(F32),
                                        ALU.subtract).then_inc(h_lo, 1)
                if d is not None:
                    prep(d + 3, n)

            experts(0, 0, True)
            with dve.Fori(1, FB) as i:
                experts(i, 0)
            with dve.Fori(1, E // 2) as pair:
                with dve.Fori(0, FB) as i:
                    experts(pair * FB + i, pair)
            add_product(STREAM["moe"] + 3 * FB * (E // 2) - 1, gain=MOD[:, 88:96])
            norm_in_place(11, 11, vec("final2"))
            for j in range(4):
                dve.wait_ge(out_turned, j + 1)
                nc.vector.tensor_copy(XIN[:, j // 2, 512 * (j % 2):512 * (j % 2) + 512],
                                      ACC[:, 512 * j:512 * j + 512]).then_inc(out_copied, 1)

        @block.tensor
        def _(pe):
            ident, ones, rot = const("ident"), const("ones"), const("rot")

            def ready(c, i=0):
                pe.wait_ge(lo_ready, i * 3 + (c + 1))

            def product(to, wh, wl, xh, xl, first, last, **kw):
                nc.tensor.matmul(to, wh, xh, start=first, stop=False, **kw)
                nc.tensor.matmul(to, wh, xl, start=False, stop=False, **kw)
                return nc.tensor.matmul(to, wl, xh, start=False, stop=last, **kw)

            def parts(c, k, n=BLOCK):
                return [w[c % RING][:, 0:n].rearrange("p (k n) -> p k n", k=k) for w in (WH, WL)]

            def tiles(bank, wh, wl, n, u=None, m=P):
                for t in range(n):
                    for k in range(DC):
                        if u is not None and t == 0:
                            pe.wait_ge(u_lo, DC * u + k + 1)
                        mm = product(bank[:, t * S:(t + 1) * S], wh[:, k, t * P:(t + 1) * P],
                                     wl[:, k, t * P:(t + 1) * P], UH[:, k, :], UL[:, k, :], k == 0, k == DC - 1)
                return mm

            def on_both_halves(to, x):
                nc.tensor.matmul(to, ident[0:ROPE, :], x, start=True, stop=False)
                return nc.tensor.matmul(to, const("swap")[0:ROPE, :], x, start=False, stop=True)

            def stats(s, free=None):
                pe.wait_ge(ss_done, s + 1)
                nc.tensor.matmul(SB[:, 0:S], ones, SS[:, 0:S], start=True, stop=False)
                nc.tensor.matmul(SB[:, 0:S], ones, SS[:, S:2 * S], start=False, stop=True).then_inc(stats_done, 1)

            def down(c, hh, hl, first, last, i=0, nk=2):
                ready(c, i)
                wh, wl = parts(c, nk)
                for f in range(DC):
                    for k in range(nk):
                        mm = product(ACC[:, f * S:(f + 1) * S], wh[:, k, f * P:(f + 1) * P], wl[:, k, f * P:(f + 1) * P],
                                     hh[:, k, :], hl[:, k, :], first and k == 0 and f % 2 == 0, last and k == nk - 1,
                                     skip_group_check=True)
                    if last and f in (1, 3, 5):
                        mm.then_inc(acc_full, 1)
                mm.then_inc(w_used, 1)

            def ffn(n, name, u, s=None, scaled=True, ada=True):
                b0, h0 = STREAM[name], FB * n

                def modulation(i):
                    pe.wait_ge(ada_landed, i * 16 + 16 * (12 * n + 1))
                    hold(pe, ada_read, i + 12 * n)
                    w = RAWA[:, :].rearrange("p (k n) -> p k n", k=DC)
                    for t in range(2):
                        for k in range(DC):
                            mm = nc.tensor.matmul(MB[:, t:t + 1], w[:, k, t * P:(t + 1) * P], CS[:, k:k + 1],
                                                  start=(k == 0), stop=(k == DC - 1))
                    mm.then_inc(ada_used, 1)

                def step(i, first=False, first_down=False):
                    g, up = (b0, b0 + 1) if first else (b0 - 1, b0)
                    ready(g, i)
                    hold(pe, g_free if scaled else silu_done, i + h0)
                    tiles(GB, *parts(g, DC), 2, u if first else None).then_inc(w_used, 1)
                    if first and s is not None:
                        stats(s)
                    ready(up, i)
                    hold(pe, u_free if scaled else h_done, i + h0)
                    tiles(UB, *parts(up, DC), 2).then_inc(w_used, 1)
                    if not first:
                        pe.wait_ge(h_lo, i + h0)
                        at = bass.ds(((i + 1) % 2) * 2, 2)
                        down(b0 + 1, HH[:, at, :], HL[:, at, :], first_down, False, i)
                    if ada:
                        modulation(i)

                step(0, True)
                step(1, first_down=True)
                with pe.Fori(2, FB) as i:
                    step(i)
                pe.wait_ge(h_lo, h0 + FB)
                at = slice((FB - 1) % 2 * 2, (FB - 1) % 2 * 2 + 2)
                down(b0 + 3 * FB - 1, HH[:, at, :], HL[:, at, :], False, True)
                if ada:
                    modulation(FB)

            def group_scores(g, qk):
                for hh in range(GH):
                    for t, (k0, k1) in enumerate(Q_TILES):
                        terms = qk(g, hh, t, k1 - k0)
                        for j, (q, k) in enumerate(terms):
                            mm = nc.tensor.matmul(ACC[:, 512 * hh + k0:512 * hh + k1], q, k,
                                                  start=(j == 0), stop=(j == len(terms) - 1))
                    mm.then_inc(at_score, 1)

            def group_outputs(g, v):
                def turn(hh):
                    pe.wait_ge(at_prob, g * GH + (hh + 1))
                    pe.wait_ge(at_pt, g * GH + (hh - 1))
                    bank = (GB, UB)[hh % 2]
                    for j in range(3):
                        mm = nc.tensor.transpose(bank[:, j * P:(j + 1) * P], PR[hh][:, j * P:(j + 1) * P], ident)
                    mm.then_inc(at_turned, 1)

                def weigh(hh):
                    pe.wait_ge(at_pt, g * GH + (hh + 1))
                    pe.wait_ge(at_ol, g * GH + (hh - 1))
                    bank = (MB, SB)[hh % 2]
                    nc.tensor.matmul(bank[:, 0:S], v(0, hh), PT[hh % 2][:, 0:S], start=True, stop=False,
                                     skip_group_check=True)
                    nc.tensor.matmul(bank[:, P:S], v(1, hh), PT[hh % 2][:, S:], start=False, stop=True,
                                     skip_group_check=True).then_inc(at_pv, 1)

                turn(0)
                turn(1)
                weigh(0)
                turn(2)
                weigh(1)
                turn(3)
                weigh(2)
                weigh(3)

            pe.wait_ge(in_const, 16)
            pe.wait_ge(in_x, 16)
            for c in range(DC):
                for t in range(TT):
                    mm = nc.tensor.transpose(ACC[:, c * S + t * P:c * S + (t + 1) * P], XIN[:, t, c * P:(c + 1) * P], ident)
                if c % 2:
                    mm.then_inc(turned, 1)
            pe.wait_ge(in_vec, 16 * N_VEC_DMAS)
            nc.tensor.transpose(MB[:, 0:NV], VR[0:NV, :], ident[0:NV, 0:NV]).then_inc(turned, 1)
            nc.tensor.transpose(SB[:, 0:NA], AR[0:NA, :], ident[0:NA, 0:NA]).then_inc(turned, 1)
            pe.wait_ge(c_ready, 1)
            ffn(0, "ffn0", 0, 0)
            stats(1)
            b = STREAM["pool"]
            ready(b)
            wh, wl = parts(b, DC)
            for g in range(4):
                pe.wait_ge(u_lo, DC + 2 * g + 2)
                for m in range(2):
                    for k in range(2):
                        mm = product(ACC[:, (2 * g + m) * S:(2 * g + m + 1) * S], wh[:, 2 * g + k, m * P:(m + 1) * P],
                                     wl[:, 2 * g + k, m * P:(m + 1) * P], UH[:, 2 * g + k, :], UL[:, 2 * g + k, :],
                                     k == 0, k == 1)
                mm.then_inc(*((acc_full, 1) if g < 3 else (w_used, 1)))
            ffn(1, "ffn1", 2, 2)
            b = STREAM["dkv"]
            ready(b)
            wh, wl = parts(b, DC, DC * (KVL + ROPE))
            for k in range(DC):
                pe.wait_ge(u_lo, DC * 3 + k + 1)
                product(GB[:, 0:S], wh[:, k, 0:P], wl[:, k, 0:P], UH[:, k, :], UL[:, k, :], k == 0, k == DC - 1)
            for k in range(DC):
                mm = product(UB[0:ROPE, 0:S], wh[:, k, P:], wl[:, k, P:], UH[:, k, :], UL[:, k, :],
                             k == 0, k == DC - 1)
            mm.then_inc(w_used, 1)
            stats(3)
            pe.wait_ge(kv_vec, 2)
            on_both_halves(GB[:, S:], T[0:ROPE, 7, :]).then_inc(kv_mm, 1)
            pe.wait_ge(kv_vec, 3)
            nc.tensor.matmul(MB[:, 0:S], rot, T[:, 2, :], start=True, stop=True).then_inc(kv_mm, 1)
            pe.wait_ge(kv_act, 1)
            nc.tensor.matmul(SB[:, 0:S], ones, T[:, 0, :], start=True, stop=True).then_inc(kv_mm, 1)
            ffn(2, "ffn2", 4)
            b = STREAM["dq"]
            ready(b)
            tiles(GB, *parts(b, DC), 2, 5).then_inc(w_used, 1)
            stats(4)
            b = STREAM["uk"]
            ready(b)
            wh, wl = parts(b, HEADS_A)
            for h in range(HEADS_A):
                if h == 8:
                    pe.wait_ge(q_act, 1)
                    nc.tensor.matmul(SB[:, 0:S], ones, T[:, 2, :], start=True, stop=False)
                    nc.tensor.matmul(SB[:, 0:S], ones, T[:, 3, :], start=False, stop=True).then_inc(q_mm, 1)
                if h % 4 == 0 and h >= 8:
                    pe.wait_ge(k_out, h // 4 - 1)
                at = (h % 8) * S
                mm = product(ACC[:, at:at + S], wh[:, h, :], wl[:, h, :], CKH[:, :], CKL[:, :], True, True)
                if h == HEADS_A - 1:
                    mm.then_inc(w_used, 1)
                elif h % 4 == 3:
                    mm.then_inc(k_full, 1)
            b = STREAM["uv"]
            ready(b)
            wh, wl = parts(b, 4)
            for j in range(8):
                pe.wait_ge(q_vec, 1) if j < 2 else pe.wait_ge(v_out, j - 1)
                t = slice(j // 4 * P, j // 4 * P + P)
                bank = (GB, UB)[j % 2]
                mm = product(bank[:, :], CKH[:, t], CKL[:, t], wh[:, j % 4, :], wl[:, j % 4, :], True, True)
                if j < 7:
                    mm.then_inc(v_full, 1)
            mm.then_inc(w_used, 1)
            pe.wait_ge(q_vec, 6)
            pe.wait_ge(k_out, 4)
            with pe.Fori(G_MLA, G_MLA + HEADS_A // GH) as g:
                for part in range(3):
                    ready(STREAM["uq"] + part, g - G_MLA)
                pe.wait_ge(at_max, g * GH)
                pe.wait_ge(at_ol, g * GH)

                def nope(k, hh, split):
                    c, at = (0, hh * NOPE) if k == 0 else (1 + hh // 2, hh % 2 * NOPE)
                    return split[(STREAM["uq"] + c) % RING][:, at:at + NOPE]

                def rotated(k, pair, split):
                    c, at = (0, GH * NOPE + pair * P) if k == 0 else (1 + pair, 2 * NOPE)
                    return split[(STREAM["uq"] + c) % RING][:, at:at + P]

                for hh in range(GH):
                    for k in range(2):
                        product(ACC[:, hh * S:(hh + 1) * S], nope(k, hh, WH),
                                nope(k, hh, WL), QCH[:, k, :], QCL[:, k, :], k == 0, k == 1)
                for pair in range(2):
                    for k in range(2):
                        mm = product(ACC[:, 1024 + pair * S:1024 + (pair + 1) * S], rotated(k, pair, WH),
                                     rotated(k, pair, WL), QCH[:, k, :], QCL[:, k, :], k == 0, k == 1)
                mm.then_inc(w_used, 3)
                pe.wait_ge(at_q, g * 2 + 2)
                nc.tensor.matmul(MB[:, :], rot, T[:, 6:8, :].rearrange("p k t -> p (k t)"),
                                 start=True, stop=True).then_inc(at_rot, 1)
                pe.wait_ge(at_qr, g + (1 - G_MLA))

                def qk(g, hh, t, n):
                    q = slice(t * P, (t + 1) * P)
                    return [(T[:, hh, q], KN[:, bass.ds(g * GH + (hh - GH * G_MLA), 1), 0:n].squeeze(1)),
                            (T[:, 4 + hh // 2, q], KRZ[:, hh % 2, 0:n])]

                group_scores(g, qk)
                pe.wait_ge(v_staged, g + (1 - G_MLA))
                group_outputs(g, lambda kb, hh: VS[:, kb, hh * P:(hh + 1) * P])
            b = STREAM["wo"]
            pe.wait_ge(at_ol, GH * G_FOX)
            down(b, OH[:, 0:2, :], OL[:, 0:2, :], True, False)
            with pe.Fori(0, 2) as i:
                for j in range(3):
                    at = bass.ds(i * 6 + (2 + 2 * j), 2)
                    down(b + 1 + j, OH[:, at, :], OL[:, at, :], False, False, i)
            down(b + 7, OH[:, 14:16, :], OL[:, 14:16, :], False, True)
            ffn(3, "ffn3", 6, 5)
            stats(6)
            stats(7)
            b = STREAM["fk"]
            ready(b)
            tiles(GB, *parts(b, DC), 2, 7).then_inc(w_used, 1)
            ready(b + 1)
            tiles(UB, *parts(b + 1, DC), 2).then_inc(w_used, 1)

            def token_major(bank, wh, wl, at, n):
                for t in range(TT):
                    for k in range(DC):
                        mm = product(bank[:, at[t]:at[t] + n], UH[:, k, t * P:(t + 1) * P], UL[:, k, t * P:(t + 1) * P],
                                     wh[:, k, :], wl[:, k, :], k == 0, k == DC - 1)
                return mm

            for g in range(2):
                for k in range(DC):
                    mm = nc.tensor.matmul(MB[0:4, g * S:(g + 1) * S], FG[:, k, 4 * g:4 * g + 4], T[:, k, :],
                                          start=(k == 0), stop=(k == DC - 1))
            mm.then_inc(fg_mm, 1)
            for j in range(2):
                ready(STREAM["fv"] + j)
                token_major(ACC, *parts(STREAM["fv"] + j, DC), (j * BW, 512 + j * BW), BW).then_inc(w_used, 1)
            pe.wait_ge(fg_vec, 3)
            for g in range(2):
                for t in range(TT):
                    at = (g * TT + t) * GH
                    mm = nc.tensor.matmul(SB[:, at:at + GH], CUM[:, g, t * P:(t + 1) * P], const("ident4")[0:4, :],
                                          start=True, stop=True)
            mm.then_inc(fg_mm, 1)
            pe.wait_ge(fg_vec, 4)
            pe.wait_ge(fg_act, 3)

            def queries(name, g, i):
                for part in range(3):
                    ready(STREAM[name] + part, i)
                pe.wait_ge(at_max, g * GH)
                pe.wait_ge(at_ol, g * GH)
                for t in range(2):
                    for part, (k0, k1) in enumerate(Q_PARTS):
                        wh, wl = parts(STREAM[name] + part, k1 - k0, (k1 - k0) * BW)
                        for k in range(k0, k1):
                            mm = product(ACC[:, t * S:(t + 1) * S], wh[:, k - k0, t * P:(t + 1) * P],
                                         wl[:, k - k0, t * P:(t + 1) * P], UH[:, k, :], UL[:, k, :], k == 0, k == DC - 1)
                mm.then_inc(w_used, 3)
                pe.wait_ge(at_q, g * 2 + 2)

            def rotate():
                nc.tensor.matmul(MB[:, :], rot, T[:, 6:8, :].rearrange("p k t -> p (k t)"),
                                 start=True, stop=True).then_inc(at_rot, 1)

            for g in range(G_FOX, G_FOX + 2):
                queries("fq", g, g - G_FOX)

                def qk(g, hh, t, n):
                    return [(T[:, 4 + hh // 2, t * P:(t + 1) * P], KZ[:, (g - G_FOX) * GH + hh, 0:n]),
                            (const("neg_ident")[0:4, hh:hh + 1].broadcast_to([4, P]), CUM[:, g - G_FOX, 0:n])]

                group_scores(g, qk)
                group_outputs(g, lambda kb, hh: V2[:, kb, ((g - G_FOX) * 2 + hh // 2) * P:((g - G_FOX) * 2 + hh // 2 + 1) * P])
            b = STREAM["skv"]
            ready(b)
            pe.wait_ge(at_ol, GH * G_WIN)
            wh, wl = parts(b, DC)
            tiles(GB, wh, wl, 1)
            token_major(GB, wh[:, :, P:], wl[:, :, P:], (S, S + P), P).then_inc(w_used, 1)
            pe.wait_ge(key_vec, 1)
            nc.tensor.matmul(MB[:, 0:S], rot, T[:, 0, :], start=True, stop=True).then_inc(key_mm, 1)
            pe.wait_ge(key_vec, 7)
            nc.tensor.matmul(UB[:, 0:S], const("swap"), T[:, 1, :], start=True, stop=True).then_inc(key_mm, 1)
            pe.wait_ge(key_vec, 8)
            for g in range(G_WIN, G_WIN + 2):
                queries("sq", g, g - G_WIN)
                rotate()
                pe.wait_ge(at_qr, g - 2)
                group_scores(g, lambda g, hh, t, n: [(T[:, 4 + hh // 2, t * P:(t + 1) * P],
                                                      KZ[:, (g - G_WIN) * 2 + hh % 2, 0:n])])
                group_outputs(g, lambda kb, hh: V2[:, kb, (g - G_WIN) * P:(g - G_WIN + 1) * P])
            b = STREAM["ewo"]
            pe.wait_ge(at_ol, GH * (G_WIN + 2))
            for j in range(4):
                down(b + j, OH[:, 2 * j:2 * j + 2, :], OL[:, 2 * j:2 * j + 2, :], j == 0, j == 3)
            stats(8)
            ffn(4, "ffn4", 8, scaled=False, ada=False)
            stats(9)
            b = STREAM["iq"]
            ready(b)
            pe.wait_ge(h_done, 5 * FB)
            tiles(GB, *parts(b, DC), 2, 9).then_inc(w_used, 1)
            ready(b + 1)
            tiles(UB, *parts(b + 1, DC), 2).then_inc(w_used, 1)
            b = STREAM["ikw"]
            ready(b)
            wh, wl = parts(b, DC, DC * (HD + IH))
            for k in range(DC):
                product(ACC[0:HD, 0:S], wh[:, k, 0:HD], wl[:, k, 0:HD], UH[:, k, :], UL[:, k, :], k == 0, k == DC - 1)
            token_major(ACC, wh[:, :, HD:], wl[:, :, HD:], (512, 512 + IH), IH).then_inc(w_used, 1)
            ready(STREAM["dk"])
            tiles(ACC[:, 1024:1536], *parts(STREAM["dk"], DC), 2).then_inc(w_used, 1)
            ready(STREAM["dv"])
            token_major(ACC, *parts(STREAM["dv"], DC), (1536, 1536 + S), BW).then_inc(w_used, 1)
            pe.wait_ge(key_vec, 12)
            nc.tensor.matmul(MB[:, :], rot, T[:, 0:2, :].rearrange("p k t -> p (k t)"), start=True, stop=True).then_inc(key_mm, 1)
            nc.tensor.matmul(SB[:, :], rot, T[:, 2:4, :].rearrange("p k t -> p (k t)"), start=True, stop=True).then_inc(key_mm, 1)
            on_both_halves(GB[:, 0:S], T[0:HD, 6, :]).then_inc(key_mm, 1)
            pe.wait_ge(key_vec, 20)
            nc.tensor.matmul(UB[:, :], rot, T[:, 4:6, :].rearrange("p k t -> p (k t)"), start=True, stop=True)
            nc.tensor.matmul(GB[:, S:], rot, T[:, 6, :], start=True, stop=True).then_inc(key_mm, 1)
            pe.wait_ge(key_vec, 21)
            nc.tensor.matmul(MB[:, :], const("swap"), T[:, 0:2, :].rearrange("p k t -> p (k t)"),
                             start=True, stop=True).then_inc(key_mm, 1)
            pe.wait_ge(key_vec, 22)
            for h in range(IH):
                hold(pe, ix_act, h - 3)
                for t, (k0, k1) in enumerate(Q_TILES):
                    mm = nc.tensor.matmul(ACC[:, 512 * (h % 4) + k0:512 * (h % 4) + k1], IQ[:, h // 2, t * P:(t + 1) * P],
                                          IKZ[:, h % 2, 0:k1 - k0], start=True, stop=True)
                mm.then_inc(ix_mm, 1)
            pe.wait_ge(ix_act, IH)
            pe.wait_ge(key_vec, 23)
            with pe.Fori(G_DSA, G_DSA + 4) as g:
                queries("dsq", g, g - G_DSA)
                rotate()
                pe.wait_ge(at_qr, g - 2)
                group_scores(g, lambda g, hh, t, n: [(T[:, 4 + hh // 2, t * P:(t + 1) * P],
                                                      KZ[:, bass.ds(g * 2 + (hh % 2 - 2 * G_DSA), 1), 0:n].squeeze(1))])
                pe.wait_ge(v_staged, g - 4)
                group_outputs(g, lambda kb, hh: VSD[:, kb, :])
            b = STREAM["owo"]
            pe.wait_ge(at_ol, GH * (G_DSA + 4))
            for j in range(4):
                down(b + j, OH[:, 2 * j:2 * j + 2, :], OL[:, 2 * j:2 * j + 2, :], j == 0, j == 3)
            stats(10)
            pe.wait_ge(u_lo, DC * 11)
            for t in range(TT):
                for k in range(DC):
                    mm = nc.tensor.matmul(MB[:, t * E:(t + 1) * E], T[:, k, t * P:(t + 1) * P], RW[:, k, :],
                                          start=(k == 0), stop=(k == DC - 1))
            mm.then_inc(rt_mm, 1)
            pe.wait_ge(rt_vec, 6)
            for e in range(E):
                for t in range(TT):
                    mm = nc.tensor.matmul(ACC[:, e * S + t * P:e * S + (t + 1) * P],
                                          COMBT[:, t, e:e + 1].broadcast_to([P, P]), ident, start=True, stop=True)
            mm.then_inc(rt_mm, 1)
            pe.wait_ge(rt_vec, 7)

            def experts(n, first=False, first_down=False):
                b0, h0, u0 = STREAM["moe"], 5 * FB, 4 * FB
                g, up = (b0, b0 + 1) if first else (b0 - 1, b0)
                ready(g, n)
                pe.wait_ge(silu_done, n + h0)
                expert_tiles(GB, g).then_inc(w_used, 1)
                ready(up, n)
                pe.wait_ge(u_free, n + u0)
                expert_tiles(UB, up).then_inc(w_used, 1)
                if not first:
                    pe.wait_ge(h_lo, n + h0)
                    at = bass.ds((n % 2) * 2, 2)
                    down(b0 + 1, HH[:, at, :], HL[:, at, :], first_down, False, n)

            def expert_tiles(bank, c):
                wh, wl = parts(c, 2 * DC)
                for j in range(2 * DC):
                    k = j % DC
                    mm = product(bank[:, j // DC * S:(j // DC + 1) * S], wh[:, j, :], wl[:, j, :], UH[:, k, :], UL[:, k, :],
                                 k == 0, k == DC - 1)
                return mm

            experts(0, True)
            experts(1, first_down=True)
            with pe.Fori(2, FB * (E // 2)) as n:
                experts(n)
            pe.wait_ge(h_lo, 5 * FB + FB * (E // 2))
            at = slice(0, 2)
            down(STREAM["moe"] + 3 * FB * (E // 2) - 1, HH[:, at, :], HL[:, at, :], False, True)
            stats(11)
            for t in range(TT):
                for c in range(DC):
                    if c == 0:
                        pe.wait_ge(*(x_ready, 52))
                    mm = nc.tensor.transpose(ACC[:, t * D + c * P:t * D + (c + 1) * P], X[:, c, t * P:(t + 1) * P], ident)
                    if c % 4 == 3:
                        mm.then_inc(out_turned, 1)


def kernel(**inputs):
    import concourse.bacc as _bacc
    from concourse.bass_utils import run_bass_kernel_spmd as _run

    nc = _bacc.Bacc("TRN2", target_bir_lowering=False, num_devices=1)
    arrays, aps = {}, {}
    given = dict(inputs, consts=constants(), window_counts=window_counts())
    for name, value in given.items():
        value = np.ascontiguousarray(value)
        arrays[f"in_{name}"] = value
        aps[name] = nc.dram_tensor(f"in_{name}", value.shape, mybir.dt.from_np(value.dtype), kind="ExternalInput").ap()
    out = nc.dram_tensor("out_0", (1, S, D), F32, kind="ExternalOutput").ap()
    two_blocks_kernel(nc, aps, out)
    r = _run(nc, [arrays], core_ids=[0])
    return r.results[0]["out_0"]
```
